# Optimizing a Trainium2 kernel written in Bass

```python
import math
import jax, jax.numpy as jnp
from jax import lax
import numpy as np

D_MODEL = 1024
BATCH = 1
SEQ = 256
DEPTH = 2

N_MIXERS = 3
N_ATTN_LAYERS = len(range(0, DEPTH, N_MIXERS))
N_CONV_LAYERS = len(range(1, DEPTH, N_MIXERS))
N_SGU_LAYERS = len(range(2, DEPTH, N_MIXERS))

ATTN_HEADS = 8
ATTN_HEAD_DIM = D_MODEL // (2 * ATTN_HEADS)
Q_BLOCK = 128
REL_BUCKETS = 32
REL_MAX_DIST = 128
CONV_WIDTH = 3
SGU_CHUNK = 128
SGU_GROUPS = 8
SGU_GROUP_DIM = D_MODEL // SGU_GROUPS
PEER_HEADS = 8
PEER_NKEYS = 128
PEER_EXPERTS = PEER_NKEYS * PEER_NKEYS
PEER_KEY_DIM = 256
PEER_HALF = PEER_KEY_DIM // 2
PEER_TOPK = 16
PEER_TOKEN_BLOCK = 128
EPS = 1e-6

kernel_name = "hybrid_diffattn_shortconv_gmlp_peer"

F32 = jnp.float32

def rmsnorm(x, g):
    xf = x.astype(F32)
    y = xf * lax.rsqrt(jnp.mean(xf * xf, axis=-1, keepdims=True) + EPS)
    return (y * g.astype(F32)).astype(x.dtype)

def rel_bucket(dist):
    n = jnp.maximum(dist, 0)
    max_exact = REL_BUCKETS // 2
    nf = jnp.maximum(n, 1).astype(F32)
    large = max_exact + (jnp.log(nf / max_exact) / math.log(REL_MAX_DIST / max_exact)
                         * (REL_BUCKETS - max_exact)).astype(jnp.int32)
    large = jnp.minimum(large, REL_BUCKETS - 1)
    return jnp.where(n < max_exact, n, large)

def lambda_init_fn(layer_idx):
    return 0.8 - 0.6 * math.exp(-0.3 * layer_idx)

def diff_attention(h, w_qkv, q_gain, k_gain, lam_q1, lam_k1, lam_q2, lam_k2, sub_gain, w_o,
                   rel_bias, lam_init):
    B, S, D = h.shape
    H, DH = ATTN_HEADS, ATTN_HEAD_DIM
    qkv = h @ w_qkv
    q = rmsnorm(qkv[..., :D].reshape(B, S, H, 2, DH), q_gain)
    k = rmsnorm(qkv[..., D:2 * D].reshape(B, S, H, 2, DH), k_gain)
    v = qkv[..., 2 * D:].reshape(B, S, H, 2 * DH)
    lam = (jnp.exp(jnp.sum(lam_q1.astype(F32) * lam_k1.astype(F32)))
           - jnp.exp(jnp.sum(lam_q2.astype(F32) * lam_k2.astype(F32))) + lam_init)
    scale = DH ** -0.5
    pos = jnp.arange(S, dtype=jnp.int32)
    outs = []
    for blk in range(S // Q_BLOCK):
        start = blk * Q_BLOCK
        end = start + Q_BLOCK
        dist = pos[start:end, None] - pos[None, :end]
        bias = jnp.transpose(rel_bias[rel_bucket(dist)], (2, 0, 1)).astype(F32)
        logits = (jnp.einsum('bqhmd,bkhmd->bhmqk', q[:, start:end], k[:, :end]).astype(F32) * scale
                  + bias[None, :, None])
        logits = jnp.where(dist >= 0, logits, -jnp.inf)
        p = jax.nn.softmax(logits, axis=-1)
        attn = (p[:, :, 0] - lam * p[:, :, 1]).astype(v.dtype)
        outs.append(jnp.einsum('bhqk,bkhe->bqhe', attn, v[:, :end]))
    o = jnp.concatenate(outs, axis=1)
    o = rmsnorm(o, sub_gain) * (1.0 - lam_init)
    return o.reshape(B, S, D) @ w_o

def short_conv(h, w_in, conv_w, w_out):
    D = h.shape[-1]
    bcx = h @ w_in
    b_gate, c_gate, xin = bcx[..., :D], bcx[..., D:2 * D], bcx[..., 2 * D:]
    z = c_gate * xin
    zc = lax.conv_general_dilated(z, conv_w[:, None, :].astype(z.dtype), window_strides=(1,),
                                  padding=[(CONV_WIDTH - 1, 0)],
                                  dimension_numbers=('NWC', 'WIO', 'NWC'),
                                  feature_group_count=D)
    return (b_gate * zc) @ w_out

def spatial_gating_mlp(h, w_in, v_gain, w_s, b_s, w_out):
    B, S, D = h.shape
    z = jax.nn.gelu(h @ w_in)
    u, v = z[..., :D], rmsnorm(z[..., D:], v_gain)
    v = v.reshape(B, S // SGU_CHUNK, SGU_CHUNK, SGU_GROUPS, SGU_GROUP_DIM)
    mask = jnp.tril(jnp.ones((SGU_CHUNK, SGU_CHUNK), dtype=bool))
    w = jnp.where(mask[None], w_s, 0.0).astype(v.dtype)
    sv = (jnp.einsum('gts,bnsgc->bntgc', w, v)
          + jnp.transpose(b_s, (1, 0))[None, None, :, :, None])
    return (u * sv.reshape(B, S, D)) @ w_out

def peer_ffn(h, w_q, sub_keys, u_tab, v_tab):
    B, S, D = h.shape
    T = B * S
    xt = h.reshape(T, D)
    q = (xt @ w_q).reshape(T, PEER_HEADS, 2, PEER_HALF)
    s = jnp.einsum('thpd,hpkd->thpk', q, sub_keys).astype(F32)
    s_top, i_top = lax.top_k(s, PEER_TOPK)
    cand = (s_top[:, :, 0, :, None] + s_top[:, :, 1, None, :]).reshape(T, PEER_HEADS, -1)
    cand_idx = (i_top[:, :, 0, :, None] * PEER_NKEYS + i_top[:, :, 1, None, :]).reshape(T, PEER_HEADS, -1)
    best, pos = lax.top_k(cand, PEER_TOPK)
    idx = jnp.take_along_axis(cand_idx, pos, axis=-1)
    gates = jax.nn.softmax(best, axis=-1)

    def expert_block(args):
        xb, ib, gb = args
        act = jnp.einsum('chkd,cd->chk', u_tab[ib], xb)
        act = (jax.nn.gelu(act.astype(F32)) * gb).astype(xb.dtype)
        return jnp.einsum('chk,chkd->cd', act, v_tab[ib])

    nb = T // PEER_TOKEN_BLOCK
    out = lax.map(expert_block, (xt.reshape(nb, PEER_TOKEN_BLOCK, D),
                                 idx.reshape(nb, PEER_TOKEN_BLOCK, PEER_HEADS, PEER_TOPK),
                                 gates.reshape(nb, PEER_TOKEN_BLOCK, PEER_HEADS, PEER_TOPK)))
    return out.reshape(B, S, D)

def setup_inputs(seed: int = 0) -> dict:
    key = jax.random.key(seed)
    ks = iter(jax.random.split(key, 32))
    D = D_MODEL
    NA, NC, NS = N_ATTN_LAYERS, N_CONV_LAYERS, N_SGU_LAYERS
    DH = ATTN_HEAD_DIM

    def nrm(shape, scale):
        return jax.random.normal(next(ks), shape, F32) * scale

    return {
        "x": nrm((BATCH, SEQ, D), 1.0),
        "rel_bias": nrm((REL_BUCKETS, ATTN_HEADS), 0.5),
        "norm_mix": 1.0 + nrm((DEPTH, D), 0.02),
        "norm_ffn": 1.0 + nrm((DEPTH, D), 0.02),
        "attn_w_qkv": nrm((NA, D, 3 * D), D ** -0.5),
        "attn_q_gain": 1.0 + nrm((NA, DH), 0.02),
        "attn_k_gain": 1.0 + nrm((NA, DH), 0.02),
        "attn_lam_q1": nrm((NA, DH), 0.1),
        "attn_lam_k1": nrm((NA, DH), 0.1),
        "attn_lam_q2": nrm((NA, DH), 0.1),
        "attn_lam_k2": nrm((NA, DH), 0.1),
        "attn_sub_gain": 1.0 + nrm((NA, 2 * DH), 0.02),
        "attn_w_o": nrm((NA, D, D), D ** -0.5),
        "conv_w_in": nrm((NC, D, 3 * D), D ** -0.5),
        "conv_w": nrm((NC, CONV_WIDTH, D), CONV_WIDTH ** -0.5),
        "conv_w_out": nrm((NC, D, D), D ** -0.5),
        "sgu_w_in": nrm((NS, D, 2 * D), D ** -0.5),
        "sgu_v_gain": 1.0 + nrm((NS, D), 0.02),
        "sgu_w_s": nrm((NS, SGU_GROUPS, SGU_CHUNK, SGU_CHUNK), SGU_CHUNK ** -0.5),
        "sgu_b_s": 1.0 + nrm((NS, SGU_GROUPS, SGU_CHUNK), 0.02),
        "sgu_w_out": nrm((NS, D, D), D ** -0.5),
        "peer_w_q": nrm((DEPTH, D, PEER_HEADS * PEER_KEY_DIM), D ** -0.5),
        "peer_keys": nrm((DEPTH, PEER_HEADS, 2, PEER_NKEYS, PEER_HALF), PEER_HALF ** -0.5),
        "peer_u": nrm((DEPTH, PEER_EXPERTS, D), D ** -0.5),
        "peer_v": nrm((DEPTH, PEER_EXPERTS, D), 0.25),
    }

def reference(x, rel_bias, norm_mix, norm_ffn,
              attn_w_qkv, attn_q_gain, attn_k_gain, attn_lam_q1, attn_lam_k1, attn_lam_q2,
              attn_lam_k2, attn_sub_gain, attn_w_o,
              conv_w_in, conv_w, conv_w_out,
              sgu_w_in, sgu_v_gain, sgu_w_s, sgu_b_s, sgu_w_out,
              peer_w_q, peer_keys, peer_u, peer_v):
    h = x
    for i in range(DEPTH):
        m, j = i % N_MIXERS, i // N_MIXERS
        hn = rmsnorm(h, norm_mix[i])
        if m == 0:
            y = diff_attention(hn, attn_w_qkv[j], attn_q_gain[j], attn_k_gain[j],
                               attn_lam_q1[j], attn_lam_k1[j], attn_lam_q2[j], attn_lam_k2[j],
                               attn_sub_gain[j], attn_w_o[j], rel_bias, lambda_init_fn(i))
        elif m == 1:
            y = short_conv(hn, conv_w_in[j], conv_w[j], conv_w_out[j])
        else:
            y = spatial_gating_mlp(hn, sgu_w_in[j], sgu_v_gain[j], sgu_w_s[j], sgu_b_s[j],
                                   sgu_w_out[j])
        h = h + y
        h = h + peer_ffn(rmsnorm(h, norm_ffn[i]), peer_w_q[i], peer_keys[i], peer_u[i], peer_v[i])
    return h


_drawn_inputs = setup_inputs


def setup_inputs(seed=0):
    import zlib

    import numpy as np

    out = dict(_drawn_inputs(seed))
    spreads = {}
    factors = {'attn_lam_q2': 2.799, 'attn_lam_k2': 5.201, 'attn_lam_k1': 2.87}
    for name, (base, spread) in spreads.items():
        noise = np.random.default_rng([zlib.crc32(name.encode()), seed]).standard_normal(out[name].shape)
        drawn = base * np.exp(spread * noise) if base else spread * noise
        out[name] = __import__('jax').numpy.asarray(drawn.astype(out[name].dtype))
    for name, factor in factors.items():
        out[name] = (out[name] * factor).astype(out[name].dtype)
    return out
```

```python
import math
from contextlib import ExitStack

import numpy as np

import concourse.bass as bass
from concourse import mybir

F32 = mybir.dt.float32
U32 = mybir.dt.uint32
I32 = mybir.dt.int32
ALU = mybir.AluOpType
ACT = mybir.ActivationFunctionType
AX = mybir.AxisListType

P = 128
D = 1024
SEQ = 256
DEPTH = 2
KT = D // P
HEADS = 8
DH = 64
BUCKETS = 32
MAX_DIST = 128
PH = 8
TOPK = 16
NKEYS = 128
EXPERTS = NKEYS * NKEYS
SLOTS = PH * TOPK
GROUP = 8
GROUPS = SLOTS // GROUP
RING = 4
WINDOWS = DEPTH * (SEQ // P)
CHUNK = 512
EPS = 1e-6
LAM_INIT = 0.8 - 0.6 * math.exp(-0.3 * 0)
FAR = 383
GELU_C = math.sqrt(2.0 / math.pi)
LOW = -3.0e38
MASKED = -1.0e30


def bucket_one_hot():
    j = np.arange(FAR + 1)
    dist = 255 - j
    n = np.maximum(dist, 0)
    exact = BUCKETS // 2
    nf = np.maximum(n, 1).astype(np.float32)
    large = exact + (np.log(nf / exact) / math.log(MAX_DIST / exact) * (BUCKETS - exact)).astype(np.int32)
    row = np.where(n < exact, n, np.minimum(large, BUCKETS - 1))
    row = np.where(dist < 0, BUCKETS, row)
    return (np.arange(BUCKETS + 1)[:, None] == row[None, :]).astype(np.float32)


def stage_uses(n):
    layer, block = divmod(n, 2)
    pp = [f"in{c}" for c in range(6)]
    tt = ["x0", "x1"]
    ss = []
    if n == 0:
        tt += [f"spread{c}" for c in range(4)]
    if layer == 0:
        tt += ["q0", "q1", "k0", "k1"]
        for c in range(2):
            ss += [f"logits{pair}{m}" for pair in (2 * c, 2 * c + 1) for m in range(2)]
            tt += [f"attn{c}{kb}" for kb in range(block + 1)]
            pp += [f"pv{c}"]
        tt += ["y0", "y1"]
    else:
        tt += ["z0", "z1", "g0", "g1"]
    pp += ["out0", "out1"]
    tt += ["f0", "f1"]
    if block == 0:
        tt += [f"keys{c}" for c in range(4)]
    for c in range(4):
        pp += [f"wq{c}"]
        tt += [f"qt{c}"]
        ss += [f"score{c}"]
    return pp, tt, ss


def stage_loads(n):
    loads = [("in", c) for c in range(6)] + [("out", c) for c in range(2)]
    if n % 2 == 0:
        loads += [("keys", 0)]
    return loads + [("wq", c) for c in range(4)]


class Pool:

    def __init__(self, banks, written, read, order):
        self.banks, self.written, self.read = banks, written, read
        self.number = {key: i for i, key in enumerate(order)}

    def bank(self, *key):
        return self.banks[self.number[key] % 2]

    def read_sem(self, *key):
        return self.read[self.number[key] % 2]

    def written_sem(self, *key):
        return self.written[self.number[key] % 2]

    def times(self, *key):
        return self.number[key] // 2


def build(nc, x, rel_bias, norm_mix, norm_ffn, w_qkv, q_gain, k_gain, lam_q1, lam_k1, lam_q2, lam_k2,
          sub_gain, w_o, conv_w_in, conv_w, conv_w_out, peer_w_q, peer_keys, peer_u, peer_v, one_hot, out):
    with ExitStack() as ctx:
        def sb(name, shape, dt=F32):
            return ctx.enter_context(nc.sbuf_tensor(name, shape, dt))

        def psum(name):
            return ctx.enter_context(nc.psum_tensor(name, [P, 512], F32))

        def sem(name):
            return ctx.enter_context(nc.semaphore(name))

        bias_dram = nc.dram_tensor("bias_by_distance", (HEADS, FAR + 1), F32, kind="Internal").ap()

        h = sb("h", [P, 2, D])
        xn = sb("xn", [P, D])
        xf = sb("xf", [P, 2, D])
        xT = sb("xT", [P, KT, P])
        yT = sb("yT", [P, KT, P])
        gain_mix = sb("gain_mix", [P, D])
        gain_ffn = sb("gain_ffn", [P, D])
        ident = sb("ident", [P, P])
        reverse = sb("reverse", [P, P])
        wring = sb("wring", [P, 2, KT * CHUNK])
        rows = sb("rows", [P, 3 * D])
        kT = sb("kT", [P, HEADS * SEQ + 16])
        vrows = sb("vrows", [P, 2, D])
        qTa = sb("qTa", [P, HEADS, P])
        bias = sb("bias", [P, HEADS, SEQ])
        ex = sb("ex", [P, 8, SEQ])
        attn = sb("attn", [P, 4, SEQ])
        aT = sb("aT", [P, 2, 4, P])
        scratch = sb("scratch", [P, 2 * D])
        qT = sb("qT", [P, 4, P])
        keysT = sb("keysT", [P, 2 * PH, NKEYS])
        score = sb("score", [P, 4, NKEYS])
        cand = sb("cand", [P, 2, TOPK, TOPK])
        pick = sb("pick", [P, 2, TOPK * TOPK])
        top = sb("top", [P, 2 * PH, TOPK])
        top_i = sb("top_i", [P, 2 * PH, TOPK], U32)
        top_f = sb("top_f", [P, 2 * PH, TOPK])
        best = sb("best", [P, PH, TOPK])
        best_e = sb("best_e", [P, PH, TOPK])
        best_s = sb("best_s", [P, PH])
        pos = sb("pos", [P, 2 * TOPK], U32)
        pos2 = sb("pos2", [P, 2, 2 * TOPK], U32)
        pos_f = sb("pos_f", [P, 2, 2 * TOPK])
        row_f = sb("row_f", [P, 2, 2 * TOPK])
        idx_f = sb("idx_f", [P, 2 * TOPK])
        idx = sb("idx", [P, WINDOWS * SLOTS], U32)
        idx_now = sb("idx_now", [P, 2, 4 * GROUP], U32)
        gates = sb("gates", [P, WINDOWS * SLOTS])
        iota_i = sb("iota_i", [P, TOPK], I32)
        iota_f = sb("iota_f", [P, TOPK])
        stat = sb("stat", [P, 32])
        root = sb("root", [P, 32])
        root_t = sb("root_t", [P, 32])
        mx = sb("mx", [P, 8])
        sums = sb("sums", [P, 8])
        lam4 = sb("lam4", [P, 4, DH])
        lam_s = sb("lam_s", [P, 2])
        neg_lam = sb("neg_lam", [P, 1])
        qg = sb("qg", [P, 2])
        subg = sb("subg", [P, P])
        cw_rows = sb("cw_rows", [24, P])
        cw = sb("cw", [P, 24])
        rel = sb("rel", [BUCKETS + 1, HEADS])
        hot = sb("hot", [BUCKETS + 1, FAR + 1])
        bias_rows = sb("bias_rows", [HEADS, FAR + 1])
        ring_u = sb("ring_u", [P, RING, D])
        ring_v = sb("ring_v", [P, RING, D])
        dots = sb("dots", [P, GROUP])
        gelu_a = sb("gelu_a", [P, GROUP])
        gelu_b = sb("gelu_b", [P, GROUP])
        gelu_e = sb("gelu_e", [P, GROUP])
        dots_g = sb("dots_g", [P, GROUP])
        weight = sb("weight", [P, GROUP])
        diag = sb("diag", [P, GROUP, P])

        acc = [psum("acc0"), psum("acc1")]
        pools = {}
        for k, name in enumerate(("pp", "tt", "ss")):
            order = [(n, what) for n in range(WINDOWS) for what in stage_uses(n)[k]]
            if name == "tt":
                order = [("start", "convw"), ("start", "bias")] + order
            pools[name] = Pool([psum(f"{name}0"), psum(f"{name}1")], [sem(f"{name}_written{i}") for i in range(2)],
                               [sem(f"{name}_read{i}") for i in range(2)], order)
        pp, tt, ss = pools["pp"], pools["tt"], pools["ss"]
        loads = [(n, *what) for n in range(WINDOWS) for what in stage_loads(n)]
        load_no = {key: i for i, key in enumerate(loads)}

        x_in = [sem("x_in0"), sem("x_in1")]
        gains_in = [sem("gains_in0"), sem("gains_in1")]
        small_in = sem("small_in")
        bias_out = sem("bias_out")
        bias_in = sem("bias_in")
        w_in = [sem("w_in0"), sem("w_in1")]
        ident_made = sem("ident_made")
        consts_made = sem("consts_made")
        xn_ready = sem("xn_ready")
        qk_ready = sem("qk_ready")
        logit_max = sem("logit_max")
        exps = sem("exps")
        attn_ready = sem("attn_ready")
        y_ready = sem("y_ready")
        yT_ready = sem("yT_ready")
        z_ready = sem("z_ready")
        score_used = sem("score_used")
        idx_ready = sem("idx_ready")
        best_ready = sem("best_ready")
        best_exp = sem("best_exp")
        lam_sum = sem("lam_sum")
        lam_exp = sem("lam_exp")
        idx_copied = sem("idx_copied")
        u_in = [sem(f"u_in{i}") for i in range(RING)]
        v_in = [sem(f"v_in{i}") for i in range(RING)]
        gather_turn = sem("gather_turn")
        dot_done = sem("dot_done")
        gelu_step = sem("gelu_step")
        gelu_arg = sem("gelu_arg")
        gelu_exp = sem("gelu_exp")
        weight_ready = sem("weight_ready")
        diag_ready = sem("diag_ready")
        v_used = sem("v_used")
        acc_read = sem("acc_read")
        h_done = sem("h_done")
        out_done = sem("out_done")
        dve_step = sem("dve_step")
        pool_step = sem("pool_step")

        x_dram = x.rearrange("a (b p) d -> (a b) p d", p=P)
        out_dram = out.rearrange("a (b p) d -> (a b) p d", p=P)
        u_dram = peer_u.rearrange("l e d -> (l e) d")
        v_dram = peer_v.rearrange("l e d -> (l e) d")
        zT = kT[:, 0:KT * (SEQ + 2)].rearrange("p (c t) -> p c t", c=KT)
        kTh = kT[:, 0:HEADS * SEQ].rearrange("p (h t) -> p h t", h=HEADS)
        in_dram = [w_qkv[0], conv_w_in[0]]
        out_w_dram = [w_o[0], conv_w_out[0]]

        def chunk_of(matrix, c):
            return matrix.rearrange("(k p) n -> p k n", p=P)[:, :, c * CHUNK:(c + 1) * CHUNK]

        def wslot(i):
            return wring[:, i % 2, :].rearrange("p (k n) -> p k n", k=KT)

        def copied(eng, pool, *keys):
            for key in keys:
                eng.wait_ge(pool.read_sem(*key), pool.times(*key) + 1)

        def written(eng, pool, *key):
            eng.wait_ge(pool.written_sem(*key), pool.times(*key) + 1)

        block = ctx.enter_context(nc.Block())

        @block.sync
        def _(sp):
            def load_weights(n):
                for what, c in stage_loads(n):
                    i = load_no[(n, what, c)]
                    if i >= 2:
                        m, was, at = loads[i - 2]
                        if was == "keys":
                            written(sp, tt, m, "keys3")
                        else:
                            written(sp, pp, m, f"{was}{at}")
                    if what == "keys":
                        dst = wring[:, i % 2, 0:2 * PH * P].rearrange("p (k d) -> p k d", d=P)
                        src = peer_keys[n // 2].rearrange("h s k d -> k (h s) d")
                    else:
                        matrix = {"in": in_dram[n // 2], "out": out_w_dram[n // 2], "wq": peer_w_q[n // 2]}[what]
                        dst, src = wslot(i), chunk_of(matrix, c)
                    sp.dma_start(dst, src).then_inc(w_in[i % 2], 16)

            sp.dma_start(h[:, 0, :], x_dram[0]).then_inc(x_in[0], 16)
            sp.dma_start(gain_mix[:, :], norm_mix[0:1, :].partition_broadcast(P)).then_inc(gains_in[0], 16)
            load_weights(0)
            load_weights(1)
            for n in (2, 3):
                load_weights(n)
            for b in range(2):
                sp.wait_ge(h_done, b + 1)
                sp.dma_start(out_dram[b], h[:, b, :]).then_inc(out_done, 16)
            sp.wait_ge(out_done, 32)

        @block.gpsimd
        def _(pool):
            nc.gpsimd.memset(ident[:, :], 0.0).then_inc(pool_step, 1)
            pool.wait_ge(pool_step, 1)
            nc.gpsimd.affine_select(out=ident[:, :], in_=ident[:, :], compare_op=ALU.not_equal, fill=1.0, base=0,
                                    pattern=[[-1, P]], channel_multiplier=1).then_inc(ident_made, 1)
            nc.gpsimd.memset(reverse[:, :], 0.0).then_inc(pool_step, 1)
            pool.wait_ge(pool_step, 2)
            nc.gpsimd.affine_select(out=reverse[:, :], in_=reverse[:, :], compare_op=ALU.not_equal, fill=1.0, base=1 - P,
                                    pattern=[[1, P]], channel_multiplier=1).then_inc(ident_made, 1)
            nc.gpsimd.iota(iota_i[:, :], [[1, TOPK]], base=0, channel_multiplier=0).then_inc(consts_made, 1)

            def gather(table, ring, used, landed, slot_no, first, column):
                if not (first and slot_no < RING):
                    pool.wait_ge(used, slot_no - (RING - 1))
                    if not isinstance(slot_no, int):
                        pool.sem_inc(gather_turn, 1)
                r = column % RING
                nc.gpsimd.indirect_dma_start(
                    ring[:, r, :], None, table,
                    bass.IndirectOffsetOnAxis(idx_now[:, column // 32, column % 32:column % 32 + 1], 0),
                ).then_inc(landed[r], 16)

            def quarter_windows(pair, first):
                for q in range(2):
                    pool.wait_ge(idx_ready, 2 * pair + (q + 1))
                    if not first:
                        for r in range(RING):
                            pool.wait_ge(v_in[r], 16 * 16 * pair + 128 * (q - 2) + 128)
                    nc.gpsimd.tensor_copy(idx_now[:, q, :], idx[:, bass.ds(64 * pair + 32 * q, 32)]).then_inc(idx_copied, 1)
                    pool.wait_ge(idx_copied, 2 * pair + (q + 1))
                    for s in range(4):
                        for j in range(GROUP):
                            column = 32 * q + GROUP * s + j
                            gather(u_dram, ring_u, dot_done, u_in, 64 * pair + column, first, column)
                            if not (first and column < GROUP):
                                gather(v_dram, ring_v, v_used, v_in, 64 * pair + (column - GROUP), first,
                                       (column - GROUP) % 64)

            quarter_windows(0, True)
            with nc.gpsimd.Fori(1, WINDOWS * SLOTS // 64) as pair:
                quarter_windows(pair, False)
            for j in range(GROUP):
                last = WINDOWS * SLOTS - GROUP + j
                gather(v_dram, ring_v, v_used, v_in, last, False, 64 - GROUP + j)

        @block.tensor
        def _(pe):
            def take(pool, *key):
                if pool.times(*key):
                    pe.wait_ge(pool.read_sem(*key), pool.times(*key))
                return pool.bank(*key)

            def project(n, what, c, src):
                i = load_no[(n, what, c)]
                pe.wait_ge(w_in[i % 2], 16 * (i // 2 + 1))
                use = f"{what}{c}"
                bank = take(pp, n, use)
                for k in range(KT):
                    mm = nc.tensor.matmul(bank[:, :], src[:, k, :], wslot(i)[:, k, :], start=(k == 0), stop=(k == KT - 1))
                mm.then_inc(pp.written_sem(n, use), 1)

            def transpose4(n, use, tiles):
                bank = take(tt, n, use)
                for j, tile in enumerate(tiles):
                    t = nc.tensor.transpose(bank[:, j * P:(j + 1) * P], tile, ident[:, :])
                t.then_inc(tt.written_sem(n, use), 1)

            def side(n, g):
                layer, b = divmod(n, 2)
                if g == 1:
                    pe.wait_ge(xn_ready, 2 * n + 1)
                    for c in range(2):
                        transpose4(n, f"x{c}", [xn[:, (4 * c + j) * P:(4 * c + j + 1) * P] for j in range(4)])
                if g == 3 and n == 0:
                    pe.wait_ge(bias_in, 16)
                    pe.wait_ge(ident_made, 2)
                    for c in range(4):
                        bank = take(tt, n, f"spread{c}")
                        nc.tensor.matmul(bank[:, :], reverse[:, :], ex[:, 2 * c:2 * c + 2, :].rearrange("p h k -> p (h k)"),
                                         start=True, stop=True).then_inc(tt.written_sem(n, f"spread{c}"), 1)
                chunks = {1: [0], 2: [1, 2], 3: [3, 4], 4: [5]}
                for c in chunks.get(g, []):
                    copied(pe, tt, (n, "x0"), (n, "x1"))
                    project(n, "in", c, xT)
                if g == 4 and layer == 0:
                    pe.wait_ge(qk_ready, n + 1)
                    for part, at in (("q", 0), ("k", D)):
                        for c in range(2):
                            transpose4(n, f"{part}{c}", [rows[:, at + (4 * c + j) * P:at + (4 * c + j + 1) * P] for j in range(4)])
                if g == 4 and layer == 1:
                    pe.wait_ge(z_ready, b + 1)
                    for part, at in (("z", D), ("g", 0)):
                        for c in range(2):
                            transpose4(n, f"{part}{c}", [rows[:, at + (4 * c + j) * P:at + (4 * c + j + 1) * P] for j in range(4)])
                if g in (5, 6) and layer == 0:
                    c = g - 5
                    nk = (b + 1) * P
                    copied(pe, tt, *((n, f"{part}{k}") for part in "qk" for k in range(2)))
                    for pair in (2 * c, 2 * c + 1):
                        for m in range(2):
                            use = f"logits{pair}{m}"
                            bank = take(ss, n, use)
                            for i in range(2):
                                mm = nc.tensor.matmul(bank[:, i * SEQ:i * SEQ + nk], qTa[m * DH:(m + 1) * DH, 2 * pair + i, :],
                                                      kTh[m * DH:(m + 1) * DH, 2 * pair + i, 0:nk], start=True, stop=True)
                            mm.then_inc(ss.written_sem(n, use), 1)
                    pe.wait_ge(attn_ready, 2 * n + c + 1)
                    for kb in range(b + 1):
                        transpose4(n, f"attn{c}{kb}", [attn[:, i, kb * P:(kb + 1) * P] for i in range(4)])
                    copied(pe, tt, *((n, f"attn{c}{kb}") for kb in range(b + 1)))
                    copied(pe, pp, (n, "in4"), (n, "in5"))
                    bank = take(pp, n, f"pv{c}")
                    for i in range(4):
                        head = 4 * c + i
                        for kb in range(b + 1):
                            mm = nc.tensor.matmul(bank[:, i * P:(i + 1) * P], aT[:, kb, i, :],
                                                  vrows[:, kb, head * P:(head + 1) * P], start=(kb == 0), stop=(kb == b))
                    mm.then_inc(pp.written_sem(n, f"pv{c}"), 1)
                if g == 7:
                    if layer == 0:
                        pe.wait_ge(y_ready, n + 1)
                        for c in range(2):
                            transpose4(n, f"y{c}", [rows[:, (4 * c + j) * P:(4 * c + j + 1) * P] for j in range(4)])
                        copied(pe, tt, (n, "y0"), (n, "y1"))
                    else:
                        pe.wait_ge(yT_ready, b + 1)
                    for c in range(2):
                        project(n, "out", c, yT)
                if g == 9:
                    pe.wait_ge(xn_ready, 2 * n + 2)
                    for c in range(2):
                        transpose4(n, f"f{c}", [xf[:, b, (4 * c + j) * P:(4 * c + j + 1) * P] for j in range(4)])
                    if b == 0:
                        i = load_no[(n, "keys", 0)]
                        pe.wait_ge(w_in[i % 2], 16 * (i // 2 + 1))
                        for c in range(4):
                            transpose4(n, f"keys{c}", [wring[:, i % 2, (4 * c + j) * P:(4 * c + j + 1) * P] for j in range(4)])
                if 9 <= g <= 12:
                    c = g - 9
                    copied(pe, tt, (n, "f0"), (n, "f1"))
                    project(n, "wq", c, xT)
                    copied(pe, pp, (n, f"wq{c}"))
                    transpose4(n, f"qt{c}", [rows[:, (4 * c + j) * P:(4 * c + j + 1) * P] for j in range(4)])
                    copied(pe, tt, (n, f"qt{c}"), (2 * layer, f"keys{c}"))
                    bank = take(ss, n, f"score{c}")
                    for j in range(4):
                        mm = nc.tensor.matmul(bank[:, j * P:(j + 1) * P], qT[:, j, :], keysT[:, 4 * c + j, :], start=True, stop=True)
                    mm.then_inc(ss.written_sem(n, f"score{c}"), 1)

            def add_experts(group, first, last):
                for j in range(GROUP):
                    pe.wait_ge(v_in[j % RING], group * 32 + 16 * (j // RING + 1))
                    pe.wait_ge(diag_ready, group * GROUP + (j + 1))
                    for half in range(2):
                        mm = nc.tensor.matmul(acc[half][:, :], diag[:, j, :], ring_v[:, j % RING, half * 512:(half + 1) * 512],
                                              start=(first and j == 0), stop=(last and j == GROUP - 1))
                    mm.then_inc(v_used, 1)

            def step(s):
                if s > 0:
                    g = s - 1
                    if g % GROUPS == 0 and g:
                        pe.wait_ge(acc_read, g // GROUPS)
                    add_experts(g, g % GROUPS == 0, g % GROUPS == GROUPS - 1)

            pe.wait_ge(ident_made, 1)
            pe.wait_ge(small_in, SMALL * 16)
            nc.tensor.transpose(tt.bank("start", "convw")[:, 0:24], cw_rows[:, :], ident[0:24, 0:24]).then_inc(
                tt.written_sem("start", "convw"), 1)
            pe.wait_ge(dve_step, 1)
            nc.tensor.matmul(tt.bank("start", "bias")[0:HEADS, 0:FAR + 1], rel[:, :], hot[:, :], start=True, stop=True).then_inc(
                tt.written_sem("start", "bias"), 1)
            for g in range(GROUPS):
                side(0, g)
            for n in range(WINDOWS - 1):
                for g in range(GROUPS):
                    step(n * GROUPS + g)
                    side(n + 1, g)
            last = (WINDOWS - 1) * GROUPS
            step(last)
            step(last + 1)
            with nc.tensor.Fori(last + 1, last + GROUPS - 1) as group:
                add_experts(group, False, False)
            step(last + GROUPS)

        @block.scalar
        def _(act):
            def side(n, g):
                layer, b = divmod(n, 2)

                def copy(pool, use, dst, scale=1.0):
                    written(act, pool, n, use)
                    src = pool.bank(n, use)[:, :]
                    if len(dst.shape) == 3:
                        src = src.rearrange("p (a c) -> p a c", a=4)
                    nc.scalar.activation(dst, src, ACT.Copy, scale=scale).then_inc(pool.read_sem(n, use), 1)

                if g == 1:
                    for c in range(2):
                        copy(tt, f"x{c}", xT[:, 4 * c:4 * c + 4, :])
                chunks = {1: [0], 2: [1, 2], 3: [3, 4], 4: [5]}
                for c in chunks.get(g, []):
                    if layer == 0 and c >= 4:
                        copy(pp, f"in{c}", vrows[:, b, (c - 4) * CHUNK:(c - 3) * CHUNK])
                    else:
                        copy(pp, f"in{c}", rows[:, c * CHUNK:(c + 1) * CHUNK])
                if g == 4 and layer == 0:
                    act.wait_ge(consts_made, 3)
                    for c in range(2):
                        copy(tt, f"q{c}", qTa[:, 4 * c:4 * c + 4, :], qg[:, 0:1])
                    for c in range(2):
                        copy(tt, f"k{c}", kTh[:, 4 * c:4 * c + 4, b * P:(b + 1) * P], qg[:, 1:2])
                if g == 4 and layer == 1:
                    for c in range(2):
                        copy(tt, f"z{c}", zT[:, 4 * c:4 * c + 4, 2 + b * P:2 + (b + 1) * P])
                    for c in range(2):
                        copy(tt, f"g{c}", qTa[:, 4 * c:4 * c + 4, :])
                if g in (5, 6) and layer == 0:
                    c = g - 5
                    nk = (b + 1) * P
                    act.wait_ge(logit_max, 2 * n + c + 1)
                    for i in range(8):
                        nc.scalar.activation(ex[:, i, 0:nk], ex[:, i, 0:nk], ACT.Exp, bias=mx[:, i:i + 1],
                                             accum_out=sums[:, i:i + 1]).then_inc(exps, 1)
                    for kb in range(b + 1):
                        copy(tt, f"attn{c}{kb}", aT[:, kb, :, :])
                    copy(pp, f"pv{c}", rows[:, c * CHUNK:(c + 1) * CHUNK])
                if g == 7 and layer == 0:
                    for c in range(2):
                        copy(tt, f"y{c}", yT[:, 4 * c:4 * c + 4, :])
                if g == 9:
                    for c in range(2):
                        copy(tt, f"f{c}", xT[:, 4 * c:4 * c + 4, :])
                    if b == 0:
                        for c in range(4):
                            copy(tt, f"keys{c}", keysT[:, 4 * c:4 * c + 4, :])
                if 9 <= g <= 12:
                    c = g - 9
                    copy(pp, f"wq{c}", rows[:, c * CHUNK:(c + 1) * CHUNK])
                    copy(tt, f"qt{c}", qT[:, :, :])
                    if 4 * n + c:
                        act.wait_ge(score_used, 4 * n + c)
                    copy(ss, f"score{c}", score[:, :, :])
                if g == 13:
                    act.wait_ge(best_ready, n + 1)
                    nc.scalar.activation(best_e[:, :, :], best_e[:, :, :], ACT.Exp).then_inc(best_exp, 1)

            def step(s):
                act.wait_ge(gelu_arg, s + 1)
                nc.scalar.activation(gelu_e[:, :], gelu_b[:, :], ACT.Exp, scale=-2.0 * GELU_C).then_inc(gelu_exp, 1)
                act.wait_ge(weight_ready, s + 1)
                for j in range(GROUP):
                    if not (isinstance(s, int) and s == 0):
                        act.wait_ge(v_used, s * GROUP + (j + 1 - GROUP))
                    nc.scalar.activation(diag[:, j, :], ident[:, :], ACT.Copy, scale=weight[:, j:j + 1]).then_inc(diag_ready, 1)

            act.dma_start(h[:, 1, :], x_dram[1]).then_inc(x_in[1], 16)
            act.dma_start(gain_ffn[:, :], norm_ffn[0:1, :].partition_broadcast(P)).then_inc(gains_in[0], 16)
            small = [(hot[:, :], one_hot), (rel[0:BUCKETS, :], rel_bias),
                     (cw_rows[:, :], conv_w[0].rearrange("w (c p) -> (w c) p", p=P)),
                     (subg[:, :], sub_gain[0:1, :].partition_broadcast(P))]
            small += [(lam4[:, i, :], v[0:1, :].partition_broadcast(P)) for i, v in enumerate((lam_q1, lam_k1, lam_q2, lam_k2))]
            for i, gain in enumerate((q_gain, k_gain)):
                for m in range(2):
                    small.append((qg[m * DH:(m + 1) * DH, i:i + 1], gain[0:1, :].rearrange("a d -> d a")))
            assert len(small) == SMALL
            for dst, src in small:
                act.dma_start(dst, src).then_inc(small_in, 16)
            act.wait_ge(lam_sum, 2)
            nc.scalar.activation(lam_s[:, :], lam_s[:, :], ACT.Exp).then_inc(lam_exp, 1)
            act.wait_ge(consts_made, 4)
            act.dma_start(bias_dram, bias_rows[:, :]).then_inc(bias_out, 16)
            act.wait_ge(bias_out, 16)
            spread = bass.AP(tensor=bias_dram.tensor, offset=0, ap=[[1, P], [FAR + 1, HEADS], [1, SEQ]])
            act.dma_start(ex[:, :, :], spread).then_inc(bias_in, 16)
            for g in range(GROUPS):
                side(0, g)
            for n in range(WINDOWS - 1):
                for g in range(GROUPS):
                    step(n * GROUPS + g)
                    side(n + 1, g)
                    if n == 1 and g == 0:
                        act.wait_ge(xn_ready, 4)
                        act.dma_start(gain_mix[:, :], norm_mix[1:2, :].partition_broadcast(P)).then_inc(gains_in[1], 16)
                        act.dma_start(gain_ffn[:, :], norm_ffn[1:2, :].partition_broadcast(P)).then_inc(gains_in[1], 16)
            with nc.scalar.Fori((WINDOWS - 1) * GROUPS, WINDOWS * GROUPS) as s:
                step(s)

        @block.vector
        def _(dve):
            done = [0]

            def link(ins):
                done[0] += 1
                ins.then_inc(dve_step, 1)
                dve.wait_ge(dve_step, done[0])

            def rms(src3, count, dim):
                sq = scratch[:, 0:count * dim].rearrange("p (c d) -> p c d", d=dim)
                link(nc.vector.tensor_tensor(sq, src3, src3, ALU.mult))
                link(nc.vector.tensor_reduce(stat[:, 0:count], sq, AX.X, ALU.add))
                link(nc.vector.tensor_scalar(stat[:, 0:count], stat[:, 0:count], 1.0 / dim, EPS, ALU.mult, ALU.add))
                v, y, t = stat[:, 0:count], root[:, 0:count], root_t[:, 0:count]
                link(nc.vector.tensor_scalar(y.bitcast(U32), v.bitcast(U32), 1, None, ALU.logical_shift_right))
                link(nc.vector.tensor_scalar(y.bitcast(U32), y.bitcast(U32), -1.0, float(0x5F3759DF), ALU.mult, ALU.add))
                for _ in range(3):
                    link(nc.vector.tensor_tensor(t, y, y, ALU.mult))
                    link(nc.vector.tensor_tensor(t, t, v, ALU.mult))
                    link(nc.vector.tensor_scalar(t, t, -0.5, 1.5, ALU.mult, ALU.add))
                    link(nc.vector.tensor_tensor(y, y, t, ALU.mult))

            def norm(b, gain, dst):
                rms(h[:, b:b + 1, :], 1, D)
                link(nc.vector.scalar_tensor_tensor(out=dst, in0=h[:, b, :], scalar=root[:, 0:1], in1=gain[:, :],
                                                    op0=ALU.mult, op1=ALU.mult))
                dve.sem_inc(xn_ready, 1)

            def finish(window):
                b = window % 2
                dve.wait_ge(v_used, SLOTS * (window + 1))
                for half in range(2):
                    hh = h[:, b, half * 512:(half + 1) * 512]
                    link(nc.vector.tensor_tensor(hh, hh, acc[half][:, :], ALU.add))
                dve.sem_inc(acc_read, 1)
                if window >= WINDOWS - 2:
                    dve.sem_inc(h_done, 1)

            def attention(n, c):
                b = n
                nk = (b + 1) * P
                first_key = SEQ - nk
                for k in range(4):
                    pair, m = 2 * c + k // 2, k % 2
                    key = (n, f"logits{pair}{m}")
                    written(dve, ss, *key)
                    src = ss.bank(*key)[:, :].rearrange("p (i k) -> p i k", i=2)[:, :, 0:nk]
                    at = 4 * (k // 2) + m
                    link(nc.vector.tensor_tensor(ex[:, at:at + 3:2, 0:nk], src,
                                                 bias[:, 2 * pair:2 * pair + 2, first_key:first_key + nk], ALU.add))
                    dve.sem_inc(ss.read_sem(*key), 1)
                link(nc.vector.tensor_reduce(mx[:, :], ex[:, :, 0:nk], AX.X, ALU.max))
                link(nc.vector.tensor_scalar(mx[:, :], mx[:, :], -1.0, None, ALU.mult))
                dve.sem_inc(logit_max, 1)
                dve.wait_ge(exps, 8 * (2 * n + c + 1))
                link(nc.vector.reciprocal(sums[:, :], sums[:, :]))
                second = sums[:, :].rearrange("p (i m) -> p i m", m=2)[:, :, 1]
                link(nc.vector.tensor_scalar(second, second, neg_lam[:, 0:1], None, ALU.mult))
                for i in range(4):
                    link(nc.vector.tensor_scalar(ex[:, 2 * i + 1, 0:nk], ex[:, 2 * i + 1, 0:nk], sums[:, 2 * i + 1:2 * i + 2], None, ALU.mult))
                    link(nc.vector.scalar_tensor_tensor(out=attn[:, i, 0:nk], in0=ex[:, 2 * i, 0:nk], scalar=sums[:, 2 * i:2 * i + 1],
                                                        in1=ex[:, 2 * i + 1, 0:nk], op0=ALU.mult, op1=ALU.add))
                dve.sem_inc(attn_ready, 1)

            def convolve(b):
                copied(dve, tt, *((2 + b, f"{part}{k}") for part in "zg" for k in range(2)))
                a = scratch[:, 0:D].rearrange("p (c t) -> p c t", c=KT)
                t = scratch[:, D:2 * D].rearrange("p (c t) -> p c t", c=KT)
                for w in range(3):
                    tap = cw[:, w * KT:(w + 1) * KT].unsqueeze(2).to_broadcast([P, KT, P])
                    link(nc.vector.tensor_tensor(a if w == 0 else t, zT[:, :, b * P + w:b * P + w + P], tap, ALU.mult))
                    if w:
                        link(nc.vector.tensor_tensor(a, a, t, ALU.add))
                link(nc.vector.tensor_tensor(yT[:, :, :], a, qTa[:, :, :], ALU.mult))
                dve.sem_inc(yT_ready, 1)

            def route(n, c):
                layer = n // 2
                copied(dve, ss, (n, f"score{c}"))
                hp = range(4 * c, 4 * c + 4)

                def top16(values, tops, indices):
                    for v, t in zip(values, tops):
                        last = nc.vector.max(t[:, 0:8], v)
                    link(last)
                    for v, t, i in zip(values, tops, indices):
                        last = nc.vector.max_index(i[:, 0:8], t[:, 0:8], v)
                    link(last)
                    for v, t in zip(values, tops):
                        last = nc.vector.match_replace(v, t[:, 0:8], v, LOW)
                    link(last)
                    for v, t in zip(values, tops):
                        last = nc.vector.max(t[:, 8:16], v)
                    link(last)
                    for v, t, i in zip(values, tops, indices):
                        last = nc.vector.max_index(i[:, 8:16], t[:, 8:16], v)
                    link(last)

                top16([score[:, j, :] for j in range(4)], [top[:, k, :] for k in hp], [top_i[:, k, :] for k in hp])
                dve.sem_inc(score_used, 1)
                link(nc.vector.tensor_copy(top_f[:, 4 * c:4 * c + 4, :], top_i[:, 4 * c:4 * c + 4, :]))
                for j in range(2):
                    s0 = top[:, 4 * c + 2 * j, :].unsqueeze(2).to_broadcast([P, TOPK, TOPK])
                    s1 = top[:, 4 * c + 2 * j + 1, :].unsqueeze(1).to_broadcast([P, TOPK, TOPK])
                    link(nc.vector.tensor_tensor(cand[:, j, :, :], s0, s1, ALU.add))
                flat = [cand[:, j, :, :].rearrange("p a c -> p (a c)") for j in range(2)]
                top16(flat, [best[:, 2 * c + j, :] for j in range(2)], [pos[:, j * TOPK:(j + 1) * TOPK] for j in range(2)])
                link(nc.vector.tensor_scalar(pos2[:, 0, :], pos[:, :], 4, None, ALU.logical_shift_right))
                link(nc.vector.tensor_scalar(pos2[:, 1, :], pos[:, :], TOPK - 1, None, ALU.bitwise_and))
                link(nc.vector.tensor_copy(pos_f[:, :, :], pos2[:, :, :]))
                for side_no in range(2):
                    one = pick[:, :, :].rearrange("p j (k a) -> p (j k) a", a=TOPK)
                    link(nc.vector.tensor_tensor(one, pos_f[:, side_no, :].unsqueeze(2).to_broadcast([P, 2 * TOPK, TOPK]),
                                                 iota_f[:, :].unsqueeze(1).to_broadcast([P, 2 * TOPK, TOPK]), ALU.is_equal))
                    for j in range(2):
                        p3 = pick[:, j, :].rearrange("p (k a) -> p k a", a=TOPK)
                        choice = top_f[:, 4 * c + 2 * j + side_no, :].unsqueeze(1).to_broadcast([P, TOPK, TOPK])
                        link(nc.vector.tensor_tensor(p3, p3, choice, ALU.mult))
                    link(nc.vector.tensor_reduce(row_f[:, side_no, :], one, AX.X, ALU.add))
                link(nc.vector.tensor_scalar(idx_f[:, :], row_f[:, 0, :], float(NKEYS), float(layer * EXPERTS), ALU.mult, ALU.add))
                link(nc.vector.tensor_tensor(idx_f[:, :], idx_f[:, :], row_f[:, 1, :], ALU.add))
                at = n * SLOTS + c * 2 * TOPK
                link(nc.vector.tensor_copy(idx[:, at:at + 2 * TOPK], idx_f[:, :]))
                dve.sem_inc(idx_ready, 1)

            def gate(n):
                link(nc.vector.tensor_tensor(best_e[:, :, :], best[:, :, :], best[:, :, 0:1].to_broadcast([P, PH, TOPK]), ALU.subtract))
                dve.sem_inc(best_ready, 1)
                dve.wait_ge(best_exp, n + 1)
                link(nc.vector.tensor_reduce(best_s[:, :], best_e[:, :, :], AX.X, ALU.add))
                link(nc.vector.reciprocal(best_s[:, :], best_s[:, :]))
                g3 = gates[:, n * SLOTS:(n + 1) * SLOTS].rearrange("p (h k) -> p h k", h=PH)
                link(nc.vector.tensor_tensor(g3, best_e[:, :, :], best_s[:, :].unsqueeze(2).to_broadcast([P, PH, TOPK]), ALU.mult))

            def side(n, g):
                layer, b = divmod(n, 2)
                if g == 0:
                    if layer:
                        finish(n - 2)
                    if layer == 0:
                        dve.wait_ge(x_in[b], 16)
                    dve.wait_ge(gains_in[layer], 32)
                    norm(b, gain_mix, xn[:, :])
                if n == 0 and g == 3:
                    for k in range(4):
                        key = (n, f"spread{k}")
                        written(dve, tt, *key)
                        link(nc.vector.tensor_copy(bias[:, 2 * k:2 * k + 2, :].rearrange("p h k -> p (h k)"), tt.bank(*key)[:, :]))
                        dve.sem_inc(tt.read_sem(*key), 1)
                if g == 4 and layer == 0:
                    copied(dve, pp, *((n, f"in{c}") for c in range(4)))
                    qk = rows[:, 0:2 * D].rearrange("p (c d) -> p c d", d=DH)
                    rms(qk, 32, DH)
                    link(nc.vector.tensor_tensor(qk, qk, root[:, 0:32].unsqueeze(2).to_broadcast([P, 32, DH]), ALU.mult))
                    dve.sem_inc(qk_ready, 1)
                if g == 4 and layer == 1:
                    if b == 0:
                        link(nc.vector.memset(zT[:, :, 0:2], 0.0))
                    copied(dve, pp, *((n, f"in{c}") for c in range(2, 6)))
                    link(nc.vector.tensor_tensor(rows[:, D:2 * D], rows[:, D:2 * D], rows[:, 2 * D:3 * D], ALU.mult))
                    dve.sem_inc(z_ready, 1)
                if g in (5, 6) and layer == 0:
                    attention(n, g - 5)
                if g == 5 and layer == 1:
                    convolve(b)
                if g == 7 and layer == 0:
                    copied(dve, pp, (n, "pv0"), (n, "pv1"))
                    o3 = rows[:, 0:D].rearrange("p (h d) -> p h d", h=HEADS)
                    rms(o3, HEADS, P)
                    link(nc.vector.tensor_tensor(o3, o3, root[:, 0:HEADS].unsqueeze(2).to_broadcast([P, HEADS, P]), ALU.mult))
                    link(nc.vector.tensor_tensor(o3, o3, subg[:, :].unsqueeze(1).to_broadcast([P, HEADS, P]), ALU.mult))
                    dve.sem_inc(y_ready, 1)
                if g == 8:
                    for c in range(2):
                        key = (n, f"out{c}")
                        written(dve, pp, *key)
                        hh = h[:, b, c * CHUNK:(c + 1) * CHUNK]
                        link(nc.vector.tensor_tensor(hh, hh, pp.bank(*key)[:, :], ALU.add))
                        dve.sem_inc(pp.read_sem(*key), 1)
                    norm(b, gain_ffn, xf[:, b, :])
                if 9 <= g <= 12:
                    route(n, g - 9)
                if g == 13:
                    gate(n)

            def step(s, b):
                fresh = isinstance(s, int) and s == 0
                for j in range(GROUP):
                    dve.wait_ge(u_in[j % RING], s * 32 + 16 * (j // RING + 1))
                    row = ring_u[:, j % RING, :]
                    nc.vector.tensor_tensor_reduce(row, row, xf[:, b, :], 1.0, 0.0, ALU.mult, ALU.add,
                                                   dots[:, j:j + 1]).then_inc(dot_done, 1)
                dve.wait_ge(dot_done, s * GROUP + GROUP)
                nc.vector.scalar_tensor_tensor(out=gelu_a[:, :], in0=dots[:, :], scalar=0.044715, in1=dots[:, :],
                                               op0=ALU.mult, op1=ALU.mult).then_inc(gelu_step, 1)
                dve.wait_ge(gelu_step, s * 5 + 1)
                nc.vector.scalar_tensor_tensor(out=gelu_b[:, :], in0=gelu_a[:, :], scalar=1.0, in1=dots[:, :],
                                               op0=ALU.add, op1=ALU.mult).then_inc(gelu_arg, 1)
                nc.vector.tensor_tensor(dots_g[:, :], dots[:, :], gates[:, bass.ds(s * GROUP, GROUP)], ALU.mult).then_inc(gelu_step, 1)
                dve.wait_ge(gelu_exp, s + 1)
                nc.vector.tensor_scalar(gelu_e[:, :], gelu_e[:, :], 1.0, None, ALU.add).then_inc(gelu_step, 1)
                dve.wait_ge(gelu_step, s * 5 + 3)
                nc.vector.reciprocal(gelu_e[:, :], gelu_e[:, :]).then_inc(gelu_step, 1)
                dve.wait_ge(gelu_step, s * 5 + 4)
                if not fresh:
                    dve.wait_ge(diag_ready, s * GROUP)
                nc.vector.tensor_tensor(weight[:, :], gelu_e[:, :], dots_g[:, :], ALU.mult).then_inc(gelu_step, 1)
                dve.wait_ge(gelu_step, s * 5 + 5)
                dve.sem_inc(weight_ready, 1)

            link(nc.vector.memset(rel[BUCKETS:BUCKETS + 1, :], MASKED))
            dve.wait_ge(consts_made, 1)
            dve.wait_ge(small_in, SMALL * 16)
            link(nc.vector.tensor_copy(iota_f[:, :], iota_i[:, :]))
            dve.sem_inc(consts_made, 1)
            link(nc.vector.tensor_scalar(qg[:, 0:1], qg[:, 0:1], DH ** -0.5, None, ALU.mult))
            dve.sem_inc(consts_made, 1)
            link(nc.vector.tensor_scalar(subg[:, :], subg[:, :], 1.0 - LAM_INIT, None, ALU.mult))
            for i in range(2):
                pair = lam4[:, 2 * i, :]
                link(nc.vector.tensor_tensor(pair, pair, lam4[:, 2 * i + 1, :], ALU.mult))
                link(nc.vector.tensor_reduce(lam_s[:, i:i + 1], pair, AX.X, ALU.add))
                dve.sem_inc(lam_sum, 1)
            dve.wait_ge(lam_exp, 1)
            link(nc.vector.tensor_tensor(neg_lam[:, :], lam_s[:, 1:2], lam_s[:, 0:1], ALU.subtract))
            link(nc.vector.tensor_scalar(neg_lam[:, :], neg_lam[:, :], -LAM_INIT, None, ALU.add))
            written(dve, tt, "start", "convw")
            link(nc.vector.tensor_copy(cw[:, :], tt.bank("start", "convw")[:, 0:24]))
            dve.sem_inc(tt.read_sem("start", "convw"), 1)
            written(dve, tt, "start", "bias")
            link(nc.vector.tensor_copy(bias_rows[:, :], tt.bank("start", "bias")[0:HEADS, 0:FAR + 1]))
            dve.sem_inc(tt.read_sem("start", "bias"), 1)
            dve.sem_inc(consts_made, 1)
            for g in range(GROUPS):
                side(0, g)
            for n in range(WINDOWS - 1):
                for g in range(GROUPS):
                    step(n * GROUPS + g, n % 2)
                    side(n + 1, g)
            step((WINDOWS - 1) * GROUPS, 1)
            finish(WINDOWS - 2)
            with nc.vector.Fori((WINDOWS - 1) * GROUPS + 1, WINDOWS * GROUPS) as s:
                step(s, 1)
            finish(WINDOWS - 1)


SMALL = 12


_INS = ['x', 'rel_bias', 'norm_mix', 'norm_ffn', 'attn_w_qkv', 'attn_q_gain', 'attn_k_gain', 'attn_lam_q1', 'attn_lam_k1',
        'attn_lam_q2', 'attn_lam_k2', 'attn_sub_gain', 'attn_w_o', 'conv_w_in', 'conv_w', 'conv_w_out', 'peer_w_q',
        'peer_keys', 'peer_u', 'peer_v']


def kernel(**inputs):
    import concourse.bacc as bacc
    from concourse.bass_utils import run_bass_kernel_spmd

    nc = bacc.Bacc("TRN2", target_bir_lowering=False, num_devices=1)
    arrays, args = {}, []
    given = {name: np.ascontiguousarray(inputs[name]) for name in _INS}
    given["one_hot"] = bucket_one_hot()
    for name, a in given.items():
        arrays[f"in_{name}_dram"] = a
        args.append(nc.dram_tensor(f"in_{name}_dram", a.shape, mybir.dt.from_np(a.dtype), kind="ExternalInput").ap())
    out = nc.dram_tensor("out_0_dram", (1, SEQ, D), F32, kind="ExternalOutput").ap()
    build(nc, *args, out)
    r = run_bass_kernel_spmd(nc, [arrays], core_ids=[0])
    return r.results[0]["out_0_dram"]
```

```python
import math
from contextlib import ExitStack

import numpy as np

import concourse.bass as bass
from concourse import mybir

F32 = mybir.dt.float32
U32 = mybir.dt.uint32
I32 = mybir.dt.int32
ALU = mybir.AluOpType
ACT = mybir.ActivationFunctionType
AX = mybir.AxisListType

P = 128
D = 1024
SEQ = 256
DEPTH = 2
KT = D // P
HEADS = 8
DH = 64
BUCKETS = 32
MAX_DIST = 128
PH = 8
TOPK = 16
NKEYS = 128
EXPERTS = NKEYS * NKEYS
SLOTS = PH * TOPK
GROUP = 8
GROUPS = SLOTS // GROUP
TICKS = 2 * GROUPS
LATE = 6
RING = 4
WINDOWS = DEPTH * (SEQ // P)
CHUNK = 512
EPS = 1e-6
LAM_INIT = 0.8 - 0.6 * math.exp(-0.3 * 0)
FAR = 383
GELU_C = math.sqrt(2.0 / math.pi)
LOW = -3.0e38
MASKED = -1.0e30


def bucket_one_hot():
    j = np.arange(FAR + 1)
    dist = 255 - j
    n = np.maximum(dist, 0)
    exact = BUCKETS // 2
    nf = np.maximum(n, 1).astype(np.float32)
    large = exact + (np.log(nf / exact) / math.log(MAX_DIST / exact) * (BUCKETS - exact)).astype(np.int32)
    row = np.where(n < exact, n, np.minimum(large, BUCKETS - 1))
    row = np.where(dist < 0, BUCKETS, row)
    return (np.arange(BUCKETS + 1)[:, None] == row[None, :]).astype(np.float32)


def stage_uses(n):
    layer, block = divmod(n, 2)
    pp = [f"in{c}" for c in range(6)]
    tt = ["x0", "x1"]
    ss = []
    if n == 0:
        tt += [f"spread{c}" for c in range(4)]
    tt += ["q0", "q1", "k0", "k1"] if layer == 0 else ["z0", "z1", "g0", "g1"]
    if block == 0:
        tt += [f"keys{c}" for c in range(4)]
    if layer == 0:
        for c in range(2):
            ss += [f"logits{pair}{m}" for pair in (2 * c, 2 * c + 1) for m in range(2)]
            tt += [f"attn{c}{kb}" for kb in range(block + 1)]
            pp += [f"pv{c}"]
        tt += ["y0", "y1"]
    pp += ["out0", "out1"]
    tt += ["f0", "f1"]
    pp += [f"wq{c}" for c in range(4)]
    tt += [f"qt{c}" for c in range(4)]
    ss += [f"score{c}" for c in range(4)]
    return pp, tt, ss


def stage_loads(n):
    keys = [("keys", 0)] if n % 2 == 0 else []
    return [("in", c) for c in range(6)] + keys + [(what, c) for what, cs in (("out", 2), ("wq", 4)) for c in range(cs)]


class Pool:

    def __init__(self, banks, written, read, order):
        self.banks, self.written, self.read = banks, written, read
        self.number = {key: i for i, key in enumerate(order)}

    def bank(self, *key):
        return self.banks[self.number[key] % 2]

    def read_sem(self, *key):
        return self.read[self.number[key] % 2]

    def written_sem(self, *key):
        return self.written[self.number[key] % 2]

    def times(self, *key):
        return self.number[key] // 2


def build(nc, x, rel_bias, norm_mix, norm_ffn, w_qkv, q_gain, k_gain, lam_q1, lam_k1, lam_q2, lam_k2,
          sub_gain, w_o, conv_w_in, conv_w, conv_w_out, peer_w_q, peer_keys, peer_u, peer_v, one_hot, out):
    with ExitStack() as ctx:
        def sb(name, shape, dt=F32):
            return ctx.enter_context(nc.sbuf_tensor(name, shape, dt))

        def psum(name):
            return ctx.enter_context(nc.psum_tensor(name, [P, 512], F32))

        def sem(name):
            return ctx.enter_context(nc.semaphore(name))

        bias_dram = nc.dram_tensor("bias_by_distance", (HEADS, FAR + 1), F32, kind="Internal").ap()

        h = sb("h", [P, 2, D])
        xn = sb("xn", [P, D])
        xf = sb("xf", [P, 2, D])
        xT = sb("xT", [P, KT, P])
        yT = sb("yT", [P, KT, P])
        gain_mix = sb("gain_mix", [P, D])
        gain_ffn = sb("gain_ffn", [P, D])
        ident = sb("ident", [P, P])
        reverse = sb("reverse", [P, P])
        wring = sb("wring", [P, 2, KT * CHUNK])
        rows = sb("rows", [P, 3 * D])
        kT = sb("kT", [P, HEADS * SEQ + 16])
        vrows = sb("vrows", [P, 2, D])
        qTa = sb("qTa", [P, HEADS, P])
        bias = sb("bias", [P, HEADS, SEQ])
        ex = sb("ex", [P, 8, SEQ])
        attn = sb("attn", [P, 4, SEQ])
        aT = sb("aT", [P, 2, 4, P])
        scratch = sb("scratch", [P, 2 * D])
        qT = sb("qT", [P, 4, P])
        keysT = sb("keysT", [P, 2 * PH, NKEYS])
        score = sb("score", [P, 4, NKEYS])
        cand = sb("cand", [P, 2, TOPK, TOPK])
        pick = sb("pick", [P, 2, TOPK * TOPK])
        top = sb("top", [P, 2 * PH, TOPK])
        top_i = sb("top_i", [P, 2 * PH, TOPK], U32)
        top_f = sb("top_f", [P, 2 * PH, TOPK])
        best = sb("best", [P, PH, TOPK])
        best_e = sb("best_e", [P, 2, TOPK])
        best_s = sb("best_s", [P, 2])
        pos = sb("pos", [P, 2 * TOPK], U32)
        pos2 = sb("pos2", [P, 2, 2 * TOPK], U32)
        pos_f = sb("pos_f", [P, 2, 2 * TOPK])
        row_f = sb("row_f", [P, 2, 2 * TOPK])
        idx_f = sb("idx_f", [P, 2 * TOPK])
        idx = sb("idx", [P, WINDOWS * SLOTS], U32)
        idx_now = sb("idx_now", [P, 2, 4 * GROUP], U32)
        gates = sb("gates", [P, WINDOWS * SLOTS])
        iota_i = sb("iota_i", [P, TOPK], I32)
        iota_f = sb("iota_f", [P, TOPK])
        stat = sb("stat", [P, 32])
        root = sb("root", [P, 32])
        root_t = sb("root_t", [P, 32])
        mx = sb("mx", [P, 8])
        sums = sb("sums", [P, 8])
        lam4 = sb("lam4", [P, 4, DH])
        lam_s = sb("lam_s", [P, 2])
        neg_lam = sb("neg_lam", [P, 1])
        qg = sb("qg", [P, 2])
        subg = sb("subg", [P, P])
        cw_rows = sb("cw_rows", [24, P])
        cw = sb("cw", [P, 24])
        rel = sb("rel", [BUCKETS + 1, HEADS])
        hot = sb("hot", [BUCKETS + 1, FAR + 1])
        bias_rows = sb("bias_rows", [HEADS, FAR + 1])
        ring_u = sb("ring_u", [P, RING, D])
        ring_v = sb("ring_v", [P, RING, D])
        dots = sb("dots", [P, GROUP])
        gelu_a = sb("gelu_a", [P, GROUP])
        gelu_b = sb("gelu_b", [P, GROUP])
        gelu_e = sb("gelu_e", [P, GROUP])
        dots_g = sb("dots_g", [P, GROUP])
        weight = sb("weight", [P, GROUP])
        diag = sb("diag", [P, GROUP, P])

        acc = [psum("acc0"), psum("acc1")]
        pools = {}
        for k, name in enumerate(("pp", "tt", "ss")):
            order = [(n, what) for n in range(WINDOWS) for what in stage_uses(n)[k]]
            if name == "tt":
                order = [("start", "convw"), ("start", "bias")] + order
            pools[name] = Pool([psum(f"{name}0"), psum(f"{name}1")], [sem(f"{name}_written{i}") for i in range(2)],
                               [sem(f"{name}_read{i}") for i in range(2)], order)
        pp, tt, ss = pools["pp"], pools["tt"], pools["ss"]
        loads = [(n, *what) for n in range(WINDOWS) for what in stage_loads(n)]
        load_no = {key: i for i, key in enumerate(loads)}

        x_in = [sem("x_in0"), sem("x_in1")]
        gains_in = [sem("gains_in0"), sem("gains_in1")]
        small_in = sem("small_in")
        bias_out = sem("bias_out")
        bias_in = sem("bias_in")
        w_in = [sem("w_in0"), sem("w_in1")]
        ident_made = sem("ident_made")
        consts_made = sem("consts_made")
        xn_ready = sem("xn_ready")
        qk_ready = sem("qk_ready")
        logit_max = sem("logit_max")
        exps = sem("exps")
        attn_ready = sem("attn_ready")
        y_ready = sem("y_ready")
        yT_ready = sem("yT_ready")
        z_ready = sem("z_ready")
        score_used = sem("score_used")
        idx_ready = sem("idx_ready")
        best_ready = sem("best_ready")
        best_exp = sem("best_exp")
        lam_sum = sem("lam_sum")
        lam_exp = sem("lam_exp")
        idx_copied = sem("idx_copied")
        u_in = [sem(f"u_in{i}") for i in range(RING)]
        v_in = [sem(f"v_in{i}") for i in range(RING)]
        gather_turn = sem("gather_turn")
        dot_done = sem("dot_done")
        gelu_step = sem("gelu_step")
        gelu_arg = sem("gelu_arg")
        gelu_exp = sem("gelu_exp")
        weight_ready = sem("weight_ready")
        diag_ready = sem("diag_ready")
        v_used = sem("v_used")
        acc_read = sem("acc_read")
        h_done = sem("h_done")
        out_done = sem("out_done")
        dve_step = sem("dve_step")
        pool_step = sem("pool_step")

        x_dram = x.rearrange("a (b p) d -> (a b) p d", p=P)
        out_dram = out.rearrange("a (b p) d -> (a b) p d", p=P)
        u_dram = peer_u.rearrange("l e d -> (l e) d")
        v_dram = peer_v.rearrange("l e d -> (l e) d")
        zT = kT[:, 0:KT * (SEQ + 2)].rearrange("p (c t) -> p c t", c=KT)
        kTh = kT[:, 0:HEADS * SEQ].rearrange("p (h t) -> p h t", h=HEADS)
        in_dram = [w_qkv[0], conv_w_in[0]]
        out_w_dram = [w_o[0], conv_w_out[0]]

        def chunk_of(matrix, c):
            return matrix.rearrange("(k p) n -> p k n", p=P)[:, :, c * CHUNK:(c + 1) * CHUNK]

        def wslot(i):
            return wring[:, i % 2, :].rearrange("p (k n) -> p k n", k=KT)

        def copied(eng, pool, *keys):
            for key in keys:
                eng.wait_ge(pool.read_sem(*key), pool.times(*key) + 1)

        def written(eng, pool, *key):
            eng.wait_ge(pool.written_sem(*key), pool.times(*key) + 1)

        block = ctx.enter_context(nc.Block())

        @block.sync
        def _(sp):
            def load_weights(n):
                for what, c in stage_loads(n):
                    i = load_no[(n, what, c)]
                    if i >= 2:
                        m, was, at = loads[i - 2]
                        if was == "keys":
                            written(sp, tt, m, "keys3")
                        else:
                            written(sp, pp, m, f"{was}{at}")
                    if what == "keys":
                        dst = wring[:, i % 2, 0:2 * PH * P].rearrange("p (k d) -> p k d", d=P)
                        src = peer_keys[n // 2].rearrange("h s k d -> k (h s) d")
                    else:
                        matrix = {"in": in_dram[n // 2], "out": out_w_dram[n // 2], "wq": peer_w_q[n // 2]}[what]
                        dst, src = wslot(i), chunk_of(matrix, c)
                    sp.dma_start(dst, src).then_inc(w_in[i % 2], 16)

            sp.dma_start(h[:, 0, :], x_dram[0]).then_inc(x_in[0], 16)
            sp.dma_start(gain_mix[:, :], norm_mix[0:1, :].partition_broadcast(P)).then_inc(gains_in[0], 16)
            load_weights(0)
            load_weights(1)
            for n in (2, 3):
                load_weights(n)
            for b in range(2):
                sp.wait_ge(h_done, b + 1)
                sp.dma_start(out_dram[b], h[:, b, :]).then_inc(out_done, 16)
            sp.wait_ge(out_done, 32)

        @block.gpsimd
        def _(pool):
            nc.gpsimd.memset(ident[:, :], 0.0).then_inc(pool_step, 1)
            pool.wait_ge(pool_step, 1)
            nc.gpsimd.affine_select(out=ident[:, :], in_=ident[:, :], compare_op=ALU.not_equal, fill=1.0, base=0,
                                    pattern=[[-1, P]], channel_multiplier=1).then_inc(ident_made, 1)
            nc.gpsimd.memset(reverse[:, :], 0.0).then_inc(pool_step, 1)
            pool.wait_ge(pool_step, 2)
            nc.gpsimd.affine_select(out=reverse[:, :], in_=reverse[:, :], compare_op=ALU.not_equal, fill=1.0, base=1 - P,
                                    pattern=[[1, P]], channel_multiplier=1).then_inc(ident_made, 1)
            nc.gpsimd.iota(iota_i[:, :], [[1, TOPK]], base=0, channel_multiplier=0).then_inc(consts_made, 1)

            def gather(table, ring, used, landed, slot_no, first, column):
                if not (first and slot_no < RING):
                    pool.wait_ge(used, slot_no - (RING - 1))
                    if not isinstance(slot_no, int):
                        pool.sem_inc(gather_turn, 1)
                r = column % RING
                nc.gpsimd.indirect_dma_start(
                    ring[:, r, :], None, table,
                    bass.IndirectOffsetOnAxis(idx_now[:, column // 32, column % 32:column % 32 + 1], 0),
                ).then_inc(landed[r], 16)

            def quarter_windows(pair, first):
                for q in range(2):
                    pool.wait_ge(idx_ready, 2 * pair + (q + 1))
                    if not first:
                        for r in range(RING):
                            pool.wait_ge(v_in[r], 16 * 16 * pair + 128 * (q - 2) + 128)
                    nc.gpsimd.tensor_copy(idx_now[:, q, :], idx[:, bass.ds(64 * pair + 32 * q, 32)]).then_inc(idx_copied, 1)
                    pool.wait_ge(idx_copied, 2 * pair + (q + 1))
                    for s in range(4):
                        for j in range(GROUP):
                            column = 32 * q + GROUP * s + j
                            gather(u_dram, ring_u, dot_done, u_in, 64 * pair + column, first, column)
                            if not (first and column < GROUP):
                                gather(v_dram, ring_v, v_used, v_in, 64 * pair + (column - GROUP), first,
                                       (column - GROUP) % 64)

            quarter_windows(0, True)
            with nc.gpsimd.Fori(1, WINDOWS * SLOTS // 64) as pair:
                quarter_windows(pair, False)
            for j in range(GROUP):
                last = WINDOWS * SLOTS - GROUP + j
                gather(v_dram, ring_v, v_used, v_in, last, False, 64 - GROUP + j)

        @block.tensor
        def _(pe):
            def take(pool, *key):
                if pool.times(*key):
                    pe.wait_ge(pool.read_sem(*key), pool.times(*key))
                return pool.bank(*key)

            def project(n, what, c, src):
                i = load_no[(n, what, c)]
                pe.wait_ge(w_in[i % 2], 16 * (i // 2 + 1))
                use = f"{what}{c}"
                bank = take(pp, n, use)
                for k in range(KT):
                    mm = nc.tensor.matmul(bank[:, :], src[:, k, :], wslot(i)[:, k, :], start=(k == 0), stop=(k == KT - 1))
                mm.then_inc(pp.written_sem(n, use), 1)

            def transpose4(n, use, tiles):
                bank = take(tt, n, use)
                for j, tile in enumerate(tiles):
                    t = nc.tensor.transpose(bank[:, j * P:(j + 1) * P], tile, ident[:, :])
                t.then_inc(tt.written_sem(n, use), 1)

            def tiles(src, first):
                return [src[:, (first + j) * P:(first + j + 1) * P] for j in range(4)]

            def logits(n, pair):
                nk = (n + 1) * P
                for m in range(2):
                    use = f"logits{pair}{m}"
                    bank = take(ss, n, use)
                    for i in range(2):
                        mm = nc.tensor.matmul(bank[:, i * SEQ:i * SEQ + nk], qTa[m * DH:(m + 1) * DH, 2 * pair + i, :],
                                              kTh[m * DH:(m + 1) * DH, 2 * pair + i, 0:nk], start=True, stop=True)
                    mm.then_inc(ss.written_sem(n, use), 1)

            def turn_attention(n, c):
                pe.wait_ge(attn_ready, 2 * n + c + 1)
                for kb in range(n + 1):
                    transpose4(n, f"attn{c}{kb}", [attn[:, i, kb * P:(kb + 1) * P] for i in range(4)])

            def mix_values(n, c):
                copied(pe, tt, *((n, f"attn{c}{kb}") for kb in range(n + 1)))
                copied(pe, pp, *((m, f"in{k}") for m in range(n + 1) for k in (4, 5)))
                bank = take(pp, n, f"pv{c}")
                for i in range(4):
                    head = 4 * c + i
                    for kb in range(n + 1):
                        mm = nc.tensor.matmul(bank[:, i * P:(i + 1) * P], aT[:, kb, i, :],
                                              vrows[:, kb, head * P:(head + 1) * P], start=(kb == 0), stop=(kb == n))
                mm.then_inc(pp.written_sem(n, f"pv{c}"), 1)

            def side(n, q):
                layer, b = divmod(n, 2)
                if q == 2:
                    pe.wait_ge(xn_ready, 2 * n + 1)
                    for c in range(2):
                        transpose4(n, f"x{c}", tiles(xn, 4 * c))
                if 2 <= q <= 7:
                    if q == 2:
                        copied(pe, tt, (n, "x0"), (n, "x1"))
                    project(n, "in", q - 2, xT)
                if q == 5 and n == 0:
                    pe.wait_ge(bias_in, 16)
                    pe.wait_ge(ident_made, 2)
                    for c in range(4):
                        bank = take(tt, n, f"spread{c}")
                        nc.tensor.matmul(bank[:, :], reverse[:, :], ex[:, 2 * c:2 * c + 2, :].rearrange("p h k -> p (h k)"),
                                         start=True, stop=True).then_inc(tt.written_sem(n, f"spread{c}"), 1)
                if q == 8 and layer == 0:
                    pe.wait_ge(qk_ready, n + 1)
                    for part, first in (("q", 0), ("k", KT)):
                        for c in range(2):
                            transpose4(n, f"{part}{c}", tiles(rows, first + 4 * c))
                if q == 9 and layer == 1:
                    pe.wait_ge(z_ready, b + 1)
                    for part, first in (("z", KT), ("g", 0)):
                        for c in range(2):
                            transpose4(n, f"{part}{c}", tiles(rows, first + 4 * c))
                if layer == 0:
                    if q in (9, 10, 12, 13):
                        if q == 9:
                            copied(pe, tt, *((n, f"{part}{k}") for part in "qk" for k in range(2)))
                        logits(n, {9: 0, 10: 1, 12: 2, 13: 3}[q])
                    if q in (13, 16):
                        turn_attention(n, (q - 13) // 3)
                    if q in (14, 17):
                        mix_values(n, (q - 14) // 3)
                if q == 19 and layer == 0:
                    pe.wait_ge(y_ready, n + 1)
                    for c in range(2):
                        transpose4(n, f"y{c}", tiles(rows, 4 * c))
                out_at = 19 if layer == 0 else 12
                if q == out_at:
                    if layer == 0:
                        copied(pe, tt, (n, "y0"), (n, "y1"))
                    else:
                        pe.wait_ge(yT_ready, b + 1)
                    project(n, "out", 0, yT)
                if q == out_at + 1:
                    project(n, "out", 1, yT)
                if q == 11 - layer and b == 0:
                    i = load_no[(n, "keys", 0)]
                    pe.wait_ge(w_in[i % 2], 16 * (i // 2 + 1))
                    for c in range(4):
                        transpose4(n, f"keys{c}", tiles(wring[:, i % 2, :], 4 * c))
                if q == 22:
                    pe.wait_ge(xn_ready, 2 * n + 2)
                    for c in range(2):
                        transpose4(n, f"f{c}", tiles(xf[:, b, :], 4 * c))
                    copied(pe, tt, (n, "f0"), (n, "f1"))
                    project(n, "wq", 0, xT)
                turn_at = {23: 0, 24: 1, 26: 2, 28: 3}
                if q in turn_at:
                    c = turn_at[q]
                    copied(pe, pp, (n, f"wq{c}"))
                    transpose4(n, f"qt{c}", tiles(rows, 4 * c))
                    if c < 3:
                        project(n, "wq", c + 1, xT)
                    copied(pe, tt, (n, f"qt{c}"), (2 * layer, f"keys{c}"))
                    bank = take(ss, n, f"score{c}")
                    for j in range(4):
                        mm = nc.tensor.matmul(bank[:, j * P:(j + 1) * P], qT[:, j, :], keysT[:, 4 * c + j, :], start=True, stop=True)
                    mm.then_inc(ss.written_sem(n, f"score{c}"), 1)

            def add_experts(group, slots, first, last):
                for j in slots:
                    pe.wait_ge(v_in[j % RING], group * 32 + 16 * (j // RING + 1))
                    pe.wait_ge(diag_ready, group * GROUP + (j + 1))
                    for half in range(2):
                        mm = nc.tensor.matmul(acc[half][:, :], diag[:, j, :], ring_v[:, j % RING, half * 512:(half + 1) * 512],
                                              start=(first and j == 0), stop=(last and j == GROUP - 1))
                    mm.then_inc(v_used, 1)

            def step(s, half):
                if s > 0:
                    g = s - 1
                    if g % GROUPS == 0 and g and half == 0:
                        pe.wait_ge(acc_read, g // GROUPS)
                    add_experts(g, HALVES[half], g % GROUPS == 0, g % GROUPS == GROUPS - 1)

            pe.wait_ge(ident_made, 1)
            pe.wait_ge(small_in, SMALL * 16)
            nc.tensor.transpose(tt.bank("start", "convw")[:, 0:24], cw_rows[:, :], ident[0:24, 0:24]).then_inc(
                tt.written_sem("start", "convw"), 1)
            pe.wait_ge(dve_step, 1)
            nc.tensor.matmul(tt.bank("start", "bias")[0:HEADS, 0:FAR + 1], rel[:, :], hot[:, :], start=True, stop=True).then_inc(
                tt.written_sem("start", "bias"), 1)
            for q in range(TICKS - LATE):
                side(0, q)
            for tick in range((WINDOWS - 1) * TICKS + LATE):
                step(tick // 2, tick % 2)
                side(*divmod(tick + TICKS - LATE, TICKS))
            alone = ((WINDOWS - 1) * TICKS + LATE) // 2
            with nc.tensor.Fori(alone - 1, WINDOWS * GROUPS - 1) as group:
                add_experts(group, range(GROUP), False, False)
            add_experts(WINDOWS * GROUPS - 1, range(GROUP), False, True)

        @block.scalar
        def _(act):
            def side(n, q):
                layer, b = divmod(n, 2)

                def copy(pool, use, dst, scale=1.0):
                    written(act, pool, n, use)
                    src = pool.bank(n, use)[:, :]
                    if len(dst.shape) == 3:
                        src = src.rearrange("p (a c) -> p a c", a=4)
                    nc.scalar.activation(dst, src, ACT.Copy, scale=scale).then_inc(pool.read_sem(n, use), 1)

                if q == 2:
                    for c in range(2):
                        copy(tt, f"x{c}", xT[:, 4 * c:4 * c + 4, :])
                if 2 <= q <= 7:
                    c = q - 2
                    if layer == 0 and c >= 4:
                        copy(pp, f"in{c}", vrows[:, b, (c - 4) * CHUNK:(c - 3) * CHUNK])
                    else:
                        copy(pp, f"in{c}", rows[:, c * CHUNK:(c + 1) * CHUNK])
                if q == 8 and layer == 0:
                    act.wait_ge(consts_made, 3)
                    for c in range(2):
                        copy(tt, f"q{c}", qTa[:, 4 * c:4 * c + 4, :], qg[:, 0:1])
                    for c in range(2):
                        copy(tt, f"k{c}", kTh[:, 4 * c:4 * c + 4, b * P:(b + 1) * P], qg[:, 1:2])
                if q == 9 and layer == 1:
                    for c in range(2):
                        copy(tt, f"z{c}", zT[:, 4 * c:4 * c + 4, 2 + b * P:2 + (b + 1) * P])
                    for c in range(2):
                        copy(tt, f"g{c}", qTa[:, 4 * c:4 * c + 4, :])
                if layer == 0:
                    if q in (11, 14):
                        c = (q - 11) // 3
                        nk = (b + 1) * P
                        act.wait_ge(logit_max, 2 * n + c + 1)
                        for i in range(8):
                            nc.scalar.activation(ex[:, i, 0:nk], ex[:, i, 0:nk], ACT.Exp, bias=mx[:, i:i + 1],
                                                 accum_out=sums[:, i:i + 1]).then_inc(exps, 1)
                    if q in (13, 16):
                        c = (q - 13) // 3
                        for kb in range(b + 1):
                            copy(tt, f"attn{c}{kb}", aT[:, kb, :, :])
                    if q in (14, 17):
                        c = (q - 14) // 3
                        copy(pp, f"pv{c}", rows[:, c * CHUNK:(c + 1) * CHUNK])
                    if q == 19:
                        for c in range(2):
                            copy(tt, f"y{c}", yT[:, 4 * c:4 * c + 4, :])
                if q == 11 - layer and b == 0:
                    for c in range(4):
                        copy(tt, f"keys{c}", keysT[:, 4 * c:4 * c + 4, :])
                if q == 22:
                    for c in range(2):
                        copy(tt, f"f{c}", xT[:, 4 * c:4 * c + 4, :])
                    copy(pp, "wq0", rows[:, 0:CHUNK])
                turn_at = {23: 0, 24: 1, 26: 2, 28: 3}
                if q in turn_at:
                    c = turn_at[q]
                    copy(tt, f"qt{c}", qT[:, :, :])
                    if c < 3:
                        copy(pp, f"wq{c + 1}", rows[:, (c + 1) * CHUNK:(c + 2) * CHUNK])
                    if 4 * n + c:
                        act.wait_ge(score_used, 4 * n + c)
                    copy(ss, f"score{c}", score[:, :, :])
                if q in (25, 27, 29, 31):
                    c = (q - 25) // 2
                    act.wait_ge(best_ready, 4 * n + c + 1)
                    nc.scalar.activation(best_e[:, :, :], best_e[:, :, :], ACT.Exp).then_inc(best_exp, 1)

            def step(s):
                act.wait_ge(gelu_arg, s + 1)
                nc.scalar.activation(gelu_e[:, :], gelu_b[:, :], ACT.Exp, scale=-2.0 * GELU_C).then_inc(gelu_exp, 1)
                act.wait_ge(weight_ready, s + 1)
                for j in range(GROUP):
                    if not (isinstance(s, int) and s == 0):
                        act.wait_ge(v_used, s * GROUP + (j + 1 - GROUP))
                    nc.scalar.activation(diag[:, j, :], ident[:, :], ACT.Copy, scale=weight[:, j:j + 1]).then_inc(diag_ready, 1)

            act.dma_start(h[:, 1, :], x_dram[1]).then_inc(x_in[1], 16)
            act.dma_start(gain_ffn[:, :], norm_ffn[0:1, :].partition_broadcast(P)).then_inc(gains_in[0], 16)
            small = [(hot[:, :], one_hot), (rel[0:BUCKETS, :], rel_bias),
                     (cw_rows[:, :], conv_w[0].rearrange("w (c p) -> (w c) p", p=P)),
                     (subg[:, :], sub_gain[0:1, :].partition_broadcast(P))]
            small += [(lam4[:, i, :], v[0:1, :].partition_broadcast(P)) for i, v in enumerate((lam_q1, lam_k1, lam_q2, lam_k2))]
            for i, gain in enumerate((q_gain, k_gain)):
                for m in range(2):
                    small.append((qg[m * DH:(m + 1) * DH, i:i + 1], gain[0:1, :].rearrange("a d -> d a")))
            assert len(small) == SMALL
            for dst, src in small:
                act.dma_start(dst, src).then_inc(small_in, 16)
            act.wait_ge(lam_sum, 2)
            nc.scalar.activation(lam_s[:, :], lam_s[:, :], ACT.Exp).then_inc(lam_exp, 1)
            act.wait_ge(consts_made, 4)
            act.dma_start(bias_dram, bias_rows[:, :]).then_inc(bias_out, 16)
            act.wait_ge(bias_out, 16)
            spread = bass.AP(tensor=bias_dram.tensor, offset=0, ap=[[1, P], [FAR + 1, HEADS], [1, SEQ]])
            act.dma_start(ex[:, :, :], spread).then_inc(bias_in, 16)
            for q in range(TICKS - LATE):
                side(0, q)
            for tick in range((WINDOWS - 1) * TICKS + LATE):
                if tick % 2:
                    step(tick // 2)
                n, q = divmod(tick + TICKS - LATE, TICKS)
                side(n, q)
                if n == 2 and q == 0:
                    act.wait_ge(xn_ready, 4)
                    act.dma_start(gain_mix[:, :], norm_mix[1:2, :].partition_broadcast(P)).then_inc(gains_in[1], 16)
                    act.dma_start(gain_ffn[:, :], norm_ffn[1:2, :].partition_broadcast(P)).then_inc(gains_in[1], 16)
            alone = ((WINDOWS - 1) * TICKS + LATE) // 2
            with nc.scalar.Fori(alone, WINDOWS * GROUPS) as s:
                step(s)

        @block.vector
        def _(dve):
            done = [0]

            def link(ins):
                done[0] += 1
                ins.then_inc(dve_step, 1)
                dve.wait_ge(dve_step, done[0])

            def rms(src3, count, dim):
                sq = scratch[:, 0:count * dim].rearrange("p (c d) -> p c d", d=dim)
                link(nc.vector.tensor_tensor(sq, src3, src3, ALU.mult))
                link(nc.vector.tensor_reduce(stat[:, 0:count], sq, AX.X, ALU.add))
                link(nc.vector.tensor_scalar(stat[:, 0:count], stat[:, 0:count], 1.0 / dim, EPS, ALU.mult, ALU.add))
                v, y, t = stat[:, 0:count], root[:, 0:count], root_t[:, 0:count]
                link(nc.vector.tensor_scalar(y.bitcast(U32), v.bitcast(U32), 1, None, ALU.logical_shift_right))
                link(nc.vector.tensor_scalar(y.bitcast(U32), y.bitcast(U32), -1.0, float(0x5F3759DF), ALU.mult, ALU.add))
                for _ in range(3):
                    link(nc.vector.tensor_tensor(t, y, y, ALU.mult))
                    link(nc.vector.tensor_tensor(t, t, v, ALU.mult))
                    link(nc.vector.tensor_scalar(t, t, -0.5, 1.5, ALU.mult, ALU.add))
                    link(nc.vector.tensor_tensor(y, y, t, ALU.mult))

            def norm(b, gain, dst):
                rms(h[:, b:b + 1, :], 1, D)
                link(nc.vector.scalar_tensor_tensor(out=dst, in0=h[:, b, :], scalar=root[:, 0:1], in1=gain[:, :],
                                                    op0=ALU.mult, op1=ALU.mult))
                dve.sem_inc(xn_ready, 1)

            def finish(window):
                b = window % 2
                dve.wait_ge(v_used, SLOTS * (window + 1))
                for half in range(2):
                    hh = h[:, b, half * 512:(half + 1) * 512]
                    link(nc.vector.tensor_tensor(hh, hh, acc[half][:, :], ALU.add))
                dve.sem_inc(acc_read, 1)
                if window >= WINDOWS - 2:
                    dve.sem_inc(h_done, 1)

            def add_bias(n, pair):
                nk = (n + 1) * P
                first_key = SEQ - nk
                for m in range(2):
                    key = (n, f"logits{pair}{m}")
                    written(dve, ss, *key)
                    src = ss.bank(*key)[:, :].rearrange("p (i k) -> p i k", i=2)[:, :, 0:nk]
                    at = 4 * (pair % 2) + m
                    link(nc.vector.tensor_tensor(ex[:, at:at + 3:2, 0:nk], src,
                                                 bias[:, 2 * pair:2 * pair + 2, first_key:first_key + nk], ALU.add))
                    dve.sem_inc(ss.read_sem(*key), 1)

            def negative_max(n):
                link(nc.vector.tensor_reduce(mx[:, :], ex[:, :, 0:(n + 1) * P], AX.X, ALU.max))
                link(nc.vector.tensor_scalar(mx[:, :], mx[:, :], -1.0, None, ALU.mult))
                dve.sem_inc(logit_max, 1)

            def difference(n, c):
                nk = (n + 1) * P
                dve.wait_ge(exps, 8 * (2 * n + c + 1))
                link(nc.vector.reciprocal(sums[:, :], sums[:, :]))
                second = sums[:, :].rearrange("p (i m) -> p i m", m=2)[:, :, 1]
                link(nc.vector.tensor_scalar(second, second, neg_lam[:, 0:1], None, ALU.mult))
                for i in range(4):
                    last = nc.vector.tensor_scalar(ex[:, 2 * i + 1, 0:nk], ex[:, 2 * i + 1, 0:nk], sums[:, 2 * i + 1:2 * i + 2], None, ALU.mult)
                link(last)
                for i in range(4):
                    last = nc.vector.scalar_tensor_tensor(out=attn[:, i, 0:nk], in0=ex[:, 2 * i, 0:nk], scalar=sums[:, 2 * i:2 * i + 1],
                                                          in1=ex[:, 2 * i + 1, 0:nk], op0=ALU.mult, op1=ALU.add)
                link(last)
                dve.sem_inc(attn_ready, 1)

            def convolve(b):
                copied(dve, tt, *((2 + b, f"{part}{k}") for part in "zg" for k in range(2)))
                a = scratch[:, 0:D].rearrange("p (c t) -> p c t", c=KT)
                t = scratch[:, D:2 * D].rearrange("p (c t) -> p c t", c=KT)
                for w in range(3):
                    tap = cw[:, w * KT:(w + 1) * KT].unsqueeze(2).to_broadcast([P, KT, P])
                    link(nc.vector.tensor_tensor(a if w == 0 else t, zT[:, :, b * P + w:b * P + w + P], tap, ALU.mult))
                    if w:
                        link(nc.vector.tensor_tensor(a, a, t, ALU.add))
                link(nc.vector.tensor_tensor(yT[:, :, :], a, qTa[:, :, :], ALU.mult))
                dve.sem_inc(yT_ready, 1)

            def top16(values, tops, indices):
                for v, t in zip(values, tops):
                    last = nc.vector.max(t[:, 0:8], v)
                link(last)
                for v, t, i in zip(values, tops, indices):
                    last = nc.vector.max_index(i[:, 0:8], t[:, 0:8], v)
                link(last)
                for v, t in zip(values, tops):
                    last = nc.vector.match_replace(v, t[:, 0:8], v, LOW)
                link(last)
                for v, t in zip(values, tops):
                    last = nc.vector.max(t[:, 8:16], v)
                link(last)
                for v, t, i in zip(values, tops, indices):
                    last = nc.vector.max_index(i[:, 8:16], t[:, 8:16], v)
                link(last)

            def best_keys(n, c):
                copied(dve, ss, (n, f"score{c}"))
                hp = range(4 * c, 4 * c + 4)
                top16([score[:, j, :] for j in range(4)], [top[:, k, :] for k in hp], [top_i[:, k, :] for k in hp])
                dve.sem_inc(score_used, 1)
                link(nc.vector.tensor_copy(top_f[:, 4 * c:4 * c + 4, :], top_i[:, 4 * c:4 * c + 4, :]))

            def best_pairs(n, c):
                layer = n // 2
                for j in range(2):
                    s0 = top[:, 4 * c + 2 * j, :].unsqueeze(2).to_broadcast([P, TOPK, TOPK])
                    s1 = top[:, 4 * c + 2 * j + 1, :].unsqueeze(1).to_broadcast([P, TOPK, TOPK])
                    link(nc.vector.tensor_tensor(cand[:, j, :, :], s0, s1, ALU.add))
                flat = [cand[:, j, :, :].rearrange("p a c -> p (a c)") for j in range(2)]
                top16(flat, [best[:, 2 * c + j, :] for j in range(2)], [pos[:, j * TOPK:(j + 1) * TOPK] for j in range(2)])
                link(nc.vector.tensor_scalar(pos2[:, 0, :], pos[:, :], 4, None, ALU.logical_shift_right))
                link(nc.vector.tensor_scalar(pos2[:, 1, :], pos[:, :], TOPK - 1, None, ALU.bitwise_and))
                link(nc.vector.tensor_copy(pos_f[:, :, :], pos2[:, :, :]))
                for side_no in range(2):
                    one = pick[:, :, :].rearrange("p j (k a) -> p (j k) a", a=TOPK)
                    link(nc.vector.tensor_tensor(one, pos_f[:, side_no, :].unsqueeze(2).to_broadcast([P, 2 * TOPK, TOPK]),
                                                 iota_f[:, :].unsqueeze(1).to_broadcast([P, 2 * TOPK, TOPK]), ALU.is_equal))
                    for j in range(2):
                        p3 = pick[:, j, :].rearrange("p (k a) -> p k a", a=TOPK)
                        choice = top_f[:, 4 * c + 2 * j + side_no, :].unsqueeze(1).to_broadcast([P, TOPK, TOPK])
                        link(nc.vector.tensor_tensor(p3, p3, choice, ALU.mult))
                    link(nc.vector.tensor_reduce(row_f[:, side_no, :], one, AX.X, ALU.add))
                link(nc.vector.tensor_scalar(idx_f[:, :], row_f[:, 0, :], float(NKEYS), float(layer * EXPERTS), ALU.mult, ALU.add))
                link(nc.vector.tensor_tensor(idx_f[:, :], idx_f[:, :], row_f[:, 1, :], ALU.add))
                at = n * SLOTS + c * 2 * TOPK
                link(nc.vector.tensor_copy(idx[:, at:at + 2 * TOPK], idx_f[:, :]))
                dve.sem_inc(idx_ready, 1)

            def gate(n, c):
                pair = best[:, 2 * c:2 * c + 2, :]
                link(nc.vector.tensor_tensor(best_e[:, :, :], pair, pair[:, :, 0:1].to_broadcast([P, 2, TOPK]), ALU.subtract))
                dve.sem_inc(best_ready, 1)
                dve.wait_ge(best_exp, 4 * n + c + 1)
                link(nc.vector.tensor_reduce(best_s[:, :], best_e[:, :, :], AX.X, ALU.add))
                link(nc.vector.reciprocal(best_s[:, :], best_s[:, :]))
                at = n * SLOTS + c * 2 * TOPK
                g3 = gates[:, at:at + 2 * TOPK].rearrange("p (h k) -> p h k", h=2)
                link(nc.vector.tensor_tensor(g3, best_e[:, :, :], best_s[:, :].unsqueeze(2).to_broadcast([P, 2, TOPK]), ALU.mult))

            def side(n, q):
                layer, b = divmod(n, 2)
                if q == 1:
                    if layer == 0:
                        dve.wait_ge(x_in[b], 16)
                    dve.wait_ge(gains_in[layer], 32)
                    norm(b, gain_mix, xn[:, :])
                if q == 5 and n == 0:
                    for c in range(4):
                        key = (n, f"spread{c}")
                        written(dve, tt, *key)
                        link(nc.vector.tensor_copy(bias[:, 2 * c:2 * c + 2, :].rearrange("p h k -> p (h k)"), tt.bank(*key)[:, :]))
                        dve.sem_inc(tt.read_sem(*key), 1)
                if layer == 0:
                    if q == 6:
                        copied(dve, pp, *((n, f"in{c}") for c in range(4)))
                        qk = rows[:, 0:2 * D].rearrange("p (c d) -> p c d", d=DH)
                        rms(qk, 32, DH)
                        link(nc.vector.tensor_tensor(qk, qk, root[:, 0:32].unsqueeze(2).to_broadcast([P, 32, DH]), ALU.mult))
                        dve.sem_inc(qk_ready, 1)
                    if q in (10, 11, 13, 14):
                        add_bias(n, {10: 0, 11: 1, 13: 2, 14: 3}[q])
                    if q in (11, 14):
                        negative_max(n)
                    if q in (12, 15):
                        difference(n, (q - 12) // 3)
                    if q == 18:
                        copied(dve, pp, (n, "pv0"), (n, "pv1"))
                        o3 = rows[:, 0:D].rearrange("p (h d) -> p h d", h=HEADS)
                        rms(o3, HEADS, P)
                        link(nc.vector.tensor_tensor(o3, o3, root[:, 0:HEADS].unsqueeze(2).to_broadcast([P, HEADS, P]), ALU.mult))
                        link(nc.vector.tensor_tensor(o3, o3, subg[:, :].unsqueeze(1).to_broadcast([P, HEADS, P]), ALU.mult))
                        dve.sem_inc(y_ready, 1)
                else:
                    if q == 8:
                        if b == 0:
                            link(nc.vector.memset(zT[:, :, 0:2], 0.0))
                        copied(dve, pp, *((n, f"in{c}") for c in range(2, 6)))
                        link(nc.vector.tensor_tensor(rows[:, D:2 * D], rows[:, D:2 * D], rows[:, 2 * D:3 * D], ALU.mult))
                        dve.sem_inc(z_ready, 1)
                    if q == 10:
                        convolve(b)
                if q == (21 if layer == 0 else 14):
                    for c in range(2):
                        key = (n, f"out{c}")
                        written(dve, pp, *key)
                        hh = h[:, b, c * CHUNK:(c + 1) * CHUNK]
                        link(nc.vector.tensor_tensor(hh, hh, pp.bank(*key)[:, :], ALU.add))
                        dve.sem_inc(pp.read_sem(*key), 1)
                    norm(b, gain_ffn, xf[:, b, :])
                if 24 <= q <= 31:
                    c = (q - 24) // 2
                    if q % 2 == 0:
                        best_keys(n, c)
                    else:
                        best_pairs(n, c)
                        gate(n, c)

            def dot(s, b, slots):
                for j in slots:
                    dve.wait_ge(u_in[j % RING], s * 32 + 16 * (j // RING + 1))
                    row = ring_u[:, j % RING, :]
                    nc.vector.tensor_tensor_reduce(row, row, xf[:, b, :], 1.0, 0.0, ALU.mult, ALU.add,
                                                   dots[:, j:j + 1]).then_inc(dot_done, 1)

            def weigh(s):
                fresh = isinstance(s, int) and s == 0
                dve.wait_ge(dot_done, s * GROUP + GROUP)
                nc.vector.scalar_tensor_tensor(out=gelu_a[:, :], in0=dots[:, :], scalar=0.044715, in1=dots[:, :],
                                               op0=ALU.mult, op1=ALU.mult).then_inc(gelu_step, 1)
                dve.wait_ge(gelu_step, s * 5 + 1)
                nc.vector.scalar_tensor_tensor(out=gelu_b[:, :], in0=gelu_a[:, :], scalar=1.0, in1=dots[:, :],
                                               op0=ALU.add, op1=ALU.mult).then_inc(gelu_arg, 1)
                nc.vector.tensor_tensor(dots_g[:, :], dots[:, :], gates[:, bass.ds(s * GROUP, GROUP)], ALU.mult).then_inc(gelu_step, 1)
                dve.wait_ge(gelu_exp, s + 1)
                nc.vector.tensor_scalar(gelu_e[:, :], gelu_e[:, :], 1.0, None, ALU.add).then_inc(gelu_step, 1)
                dve.wait_ge(gelu_step, s * 5 + 3)
                nc.vector.reciprocal(gelu_e[:, :], gelu_e[:, :]).then_inc(gelu_step, 1)
                dve.wait_ge(gelu_step, s * 5 + 4)
                if not fresh:
                    dve.wait_ge(diag_ready, s * GROUP)
                nc.vector.tensor_tensor(weight[:, :], gelu_e[:, :], dots_g[:, :], ALU.mult).then_inc(gelu_step, 1)
                dve.wait_ge(gelu_step, s * 5 + 5)
                dve.sem_inc(weight_ready, 1)

            link(nc.vector.memset(rel[BUCKETS:BUCKETS + 1, :], MASKED))
            dve.wait_ge(consts_made, 1)
            dve.wait_ge(small_in, SMALL * 16)
            link(nc.vector.tensor_copy(iota_f[:, :], iota_i[:, :]))
            dve.sem_inc(consts_made, 1)
            link(nc.vector.tensor_scalar(qg[:, 0:1], qg[:, 0:1], DH ** -0.5, None, ALU.mult))
            dve.sem_inc(consts_made, 1)
            link(nc.vector.tensor_scalar(subg[:, :], subg[:, :], 1.0 - LAM_INIT, None, ALU.mult))
            for i in range(2):
                pair = lam4[:, 2 * i, :]
                link(nc.vector.tensor_tensor(pair, pair, lam4[:, 2 * i + 1, :], ALU.mult))
                link(nc.vector.tensor_reduce(lam_s[:, i:i + 1], pair, AX.X, ALU.add))
                dve.sem_inc(lam_sum, 1)
            dve.wait_ge(lam_exp, 1)
            link(nc.vector.tensor_tensor(neg_lam[:, :], lam_s[:, 1:2], lam_s[:, 0:1], ALU.subtract))
            link(nc.vector.tensor_scalar(neg_lam[:, :], neg_lam[:, :], -LAM_INIT, None, ALU.add))
            written(dve, tt, "start", "convw")
            link(nc.vector.tensor_copy(cw[:, :], tt.bank("start", "convw")[:, 0:24]))
            dve.sem_inc(tt.read_sem("start", "convw"), 1)
            written(dve, tt, "start", "bias")
            link(nc.vector.tensor_copy(bias_rows[:, :], tt.bank("start", "bias")[0:HEADS, 0:FAR + 1]))
            dve.sem_inc(tt.read_sem("start", "bias"), 1)
            dve.sem_inc(consts_made, 1)
            for q in range(TICKS - LATE):
                side(0, q)
            for tick in range((WINDOWS - 1) * TICKS + LATE):
                s, half = divmod(tick, 2)
                dot(s, (s // GROUPS) % 2, HALVES[half])
                if half:
                    weigh(s)
                if tick % TICKS == 1 and s:
                    finish(s // GROUPS - 1)
                side(*divmod(tick + TICKS - LATE, TICKS))
            alone = ((WINDOWS - 1) * TICKS + LATE) // 2
            with nc.vector.Fori(alone, WINDOWS * GROUPS) as s:
                dot(s, 1, range(GROUP))
                weigh(s)
            finish(WINDOWS - 1)


HALVES = (range(0, GROUP // 2), range(GROUP // 2, GROUP))
SMALL = 12


_INS = ['x', 'rel_bias', 'norm_mix', 'norm_ffn', 'attn_w_qkv', 'attn_q_gain', 'attn_k_gain', 'attn_lam_q1', 'attn_lam_k1',
        'attn_lam_q2', 'attn_lam_k2', 'attn_sub_gain', 'attn_w_o', 'conv_w_in', 'conv_w', 'conv_w_out', 'peer_w_q',
        'peer_keys', 'peer_u', 'peer_v']


def kernel(**inputs):
    import concourse.bacc as bacc
    from concourse.bass_utils import run_bass_kernel_spmd

    nc = bacc.Bacc("TRN2", target_bir_lowering=False, num_devices=1)
    arrays, args = {}, []
    given = {name: np.ascontiguousarray(inputs[name]) for name in _INS}
    given["one_hot"] = bucket_one_hot()
    for name, a in given.items():
        arrays[f"in_{name}_dram"] = a
        args.append(nc.dram_tensor(f"in_{name}_dram", a.shape, mybir.dt.from_np(a.dtype), kind="ExternalInput").ap())
    out = nc.dram_tensor("out_0_dram", (1, SEQ, D), F32, kind="ExternalOutput").ap()
    build(nc, *args, out)
    r = run_bass_kernel_spmd(nc, [arrays], core_ids=[0])
    return r.results[0]["out_0_dram"]
```

```python
import math
from contextlib import ExitStack

import numpy as np

import concourse.bass as bass
from concourse import mybir

F32 = mybir.dt.float32
U32 = mybir.dt.uint32
I32 = mybir.dt.int32
ALU = mybir.AluOpType
ACT = mybir.ActivationFunctionType
AX = mybir.AxisListType

P = 128
D = 1024
SEQ = 256
DEPTH = 2
KT = D // P
HEADS = 8
DH = 64
BUCKETS = 32
MAX_DIST = 128
PH = 8
TOPK = 16
NKEYS = 128
EXPERTS = NKEYS * NKEYS
SLOTS = PH * TOPK
GROUP = 8
GROUPS = SLOTS // GROUP
TICKS = 2 * GROUPS
LATE = 6
TAIL = 5
RING = 4
WINDOWS = DEPTH * (SEQ // P)
KEPT = (0, 2, 4)
CHUNK = 512
EPS = 1e-6
LAM_INIT = 0.8 - 0.6 * math.exp(-0.3 * 0)
FAR = 383
GELU_C = math.sqrt(2.0 / math.pi)
LOW = -3.0e38
MASKED = -1.0e30


def bucket_one_hot():
    j = np.arange(FAR + 1)
    dist = 255 - j
    n = np.maximum(dist, 0)
    exact = BUCKETS // 2
    nf = np.maximum(n, 1).astype(np.float32)
    large = exact + (np.log(nf / exact) / math.log(MAX_DIST / exact) * (BUCKETS - exact)).astype(np.int32)
    row = np.where(n < exact, n, np.minimum(large, BUCKETS - 1))
    row = np.where(dist < 0, BUCKETS, row)
    return (np.arange(BUCKETS + 1)[:, None] == row[None, :]).astype(np.float32)


def uses(n):
    layer, block = divmod(n, 2)

    def of(m, *names):
        return [(m, name) for name in names]

    keys = of(n, *(f"keys{c}" for c in range(4))) if block == 0 else []
    ss = []
    if layer == 0:
        tt = of(n, "q0", "q1", "k0", "k1")
        for c in range(2):
            ss += of(n, *(f"logits{pair}{m}" for pair in (2 * c, 2 * c + 1) for m in range(2)))
            tt += of(n, *(f"attn{c}{kb}" for kb in range(block + 1)))
        tt += of(n, "y0", "y1") + keys if n == 0 else keys + of(n, "y0", "y1")
        pp = of(n, "pv0", "pv1")
    else:
        tt = of(n, "x0", "x1", "z0", "z1", "g0", "g1") + keys
        pp = of(n, *(f"in{c}" for c in range(6)))
    if n == 0:
        tt = of(0, "x0", "x1", "convw", "bias") + of(1, "x0", "x1") + of(0, "spread0", "spread1", "spread2", "spread3") + tt
        pp = (of(0, "in0", "in1", "in2", "in3") + of(1, "in0", "in1") + of(0, "in4", "in5", "pv0") + of(1, "in2")
              + of(0, "pv1") + of(1, "in3", "in4") + of(0, "out0", "out1") + of(1, "in5"))
    else:
        pp += of(n, "out0", "out1")
    pp += of(n, "wq0", "wq1", "wq2", "wq3")
    tt += of(n, "f0", "f1", "qt0", "qt1", "qt2", "qt3")
    ss += of(n, "score0", "score1", "score2", "score3")
    return pp, tt, ss


def weight_loads():
    first = [("in", 0), ("in", 1), ("in", 2), ("in", 3), ("in", 4), ("in", 5), ("out", 0), ("out", 1), ("keys", 0),
             ("wq", 0), ("wq", 1), ("wq", 2), ("wq", 3)]
    loads = [(0, *what, place) for what, place in zip(first, (0, 1, 2, 3, 0, 1, 2, 3, 0, 2, 1, 0, 1))]
    later = []
    for n in range(1, WINDOWS):
        if n > 1:
            later += [(n, "in", c) for c in range(6) if not (n == 3 and c in KEPT)]
        if n % 2 == 0:
            later.append((n, "keys", 0))
        later += [(n, what, c) for what, cs in (("out", 2), ("wq", 4)) for c in range(cs)]
    ring_no = 0
    for what in later:
        if what[0] == 2 and what[1] == "in" and what[2] in KEPT:
            loads.append((*what, 4 + KEPT.index(what[2])))
        else:
            loads.append((*what, ring_no % 2))
            ring_no += 1
    return loads


class Pool:

    def __init__(self, banks, written, read, order):
        self.banks, self.written, self.read = banks, written, read
        self.number = {key: i for i, key in enumerate(order)}

    def bank(self, *key):
        return self.banks[self.number[key] % 2]

    def read_sem(self, *key):
        return self.read[self.number[key] % 2]

    def written_sem(self, *key):
        return self.written[self.number[key] % 2]

    def times(self, *key):
        return self.number[key] // 2


def build(nc, x, rel_bias, norm_mix, norm_ffn, w_qkv, q_gain, k_gain, lam_q1, lam_k1, lam_q2, lam_k2,
          sub_gain, w_o, conv_w_in, conv_w, conv_w_out, peer_w_q, peer_keys, peer_u, peer_v, one_hot, out):
    with ExitStack() as ctx:
        def sb(name, shape, dt=F32):
            return ctx.enter_context(nc.sbuf_tensor(name, shape, dt))

        def psum(name):
            return ctx.enter_context(nc.psum_tensor(name, [P, 512], F32))

        def sem(name):
            return ctx.enter_context(nc.semaphore(name))

        bias_dram = nc.dram_tensor("bias_by_distance", (HEADS, FAR + 1), F32, kind="Internal").ap()

        h = sb("h", [P, 2, D])
        xf = sb("xf", [P, 2, D])
        xT = sb("xT", [P, KT, P])
        yT = xT
        gain_mix = sb("gain_mix", [P, D])
        gain_ffn = sb("gain_ffn", [P, D])
        ident = sb("ident", [P, P])
        reverse = sb("reverse", [P, P])
        wring = sb("wring", [P, 2, KT * CHUNK])
        rows = sb("rows", [P, 3 * D])
        room = sb("room", [P, len(KEPT), KT * CHUNK])

        def part(which, at, size, pattern=None, **sizes):
            view = room[:, which, at:at + size]
            return view.rearrange(pattern, **sizes) if pattern else view

        rows1 = part(0, 0, 2 * D)
        vrows = part(0, 2 * D, 2 * D, "p (b d) -> p b d", b=2)
        bias = part(1, 0, HEADS * SEQ, "p (h k) -> p h k", h=HEADS)
        ex = part(1, HEADS * SEQ, 8 * SEQ, "p (i k) -> p i k", i=8)
        attn = part(2, 0, 4 * SEQ, "p (i k) -> p i k", i=4)
        aT = part(2, 4 * SEQ, 8 * P, "p (b i q) -> p b i q", b=2, i=4)
        kT = sb("kT", [P, HEADS * SEQ + 16])
        qTa = sb("qTa", [P, HEADS, P])
        attn_flat = part(2, 0, 4 * SEQ)
        hot = attn_flat[0:BUCKETS + 1, 0:FAR + 1]
        bias_rows = attn_flat[0:HEADS, 2 * SEQ:2 * SEQ + FAR + 1]
        scratch = sb("scratch", [P, 2 * D])
        xn = scratch[:, D:2 * D]
        qT = sb("qT", [P, 4, P])
        keysT = sb("keysT", [P, 2 * PH, NKEYS])
        score = sb("score", [P, 2, 4, NKEYS])
        cand = sb("cand", [P, 2, TOPK, TOPK])
        pick = sb("pick", [P, 2, TOPK * TOPK])
        top = sb("top", [P, 2 * PH, TOPK])
        top_i = sb("top_i", [P, 2 * PH, TOPK], U32)
        top_f = sb("top_f", [P, 2 * PH, TOPK])
        best = sb("best", [P, PH, TOPK])
        best_e = sb("best_e", [P, 2, TOPK])
        best_s = sb("best_s", [P, 2])
        pos = sb("pos", [P, 2 * TOPK], U32)
        pos2 = sb("pos2", [P, 2, 2 * TOPK], U32)
        pos_f = sb("pos_f", [P, 2, 2 * TOPK])
        row_f = sb("row_f", [P, 2, 2 * TOPK])
        idx_f = sb("idx_f", [P, 2 * TOPK])
        idx = sb("idx", [P, WINDOWS * SLOTS], U32)
        idx_now = sb("idx_now", [P, 2, 4 * GROUP], U32)
        gates = sb("gates", [P, WINDOWS * SLOTS])
        iota_i = sb("iota_i", [P, TOPK], I32)
        iota_f = sb("iota_f", [P, TOPK])
        stat = sb("stat", [P, 32])
        root = sb("root", [P, 32])
        root_t = sb("root_t", [P, 32])
        mx = sb("mx", [P, 8])
        sums = sb("sums", [P, 8])
        lam4 = sb("lam4", [P, 4, DH])
        lam_s = sb("lam_s", [P, 2])
        neg_lam = sb("neg_lam", [P, 1])
        qg = sb("qg", [P, 2])
        subg = sb("subg", [P, P])
        cw_rows = sb("cw_rows", [24, P])
        cw = sb("cw", [P, 24])
        rel = sb("rel", [BUCKETS + 1, HEADS])
        ring_u = sb("ring_u", [P, RING, D])
        ring_v = sb("ring_v", [P, RING, D])
        dots = sb("dots", [P, GROUP])
        gelu_a = sb("gelu_a", [P, GROUP])
        gelu_b = sb("gelu_b", [P, GROUP])
        gelu_e = sb("gelu_e", [P, GROUP])
        dots_g = sb("dots_g", [P, GROUP])
        weight = sb("weight", [P, GROUP])
        diag = sb("diag", [P, GROUP, P])

        acc = [psum("acc0"), psum("acc1")]
        pools = {}
        for k, name in enumerate(("pp", "tt", "ss")):
            order = [use for n in range(WINDOWS) for use in uses(n)[k]]
            pools[name] = Pool([psum(f"{name}0"), psum(f"{name}1")], [sem(f"{name}_written{i}") for i in range(2)],
                               [sem(f"{name}_read{i}") for i in range(2)], order)
        pp, tt, ss = pools["pp"], pools["tt"], pools["ss"]
        loads = weight_loads()
        held_at = {}
        for place in range(4 + len(KEPT)):
            for i, load in enumerate(load for load in loads if load[3] == place):
                held_at[load[:3]] = place, i

        x_in = [sem("x_in0"), sem("x_in1")]
        mix_gain_in = sem("mix_gain_in")
        ffn_gain_in = sem("ffn_gain_in")
        small_in = sem("small_in")
        bias_out = sem("bias_out")
        bias_in = sem("bias_in")
        w_in = [sem(f"w_in{i}") for i in range(4 + len(KEPT))]
        ident_made = sem("ident_made")
        consts_made = sem("consts_made")
        xn_ready = sem("xn_ready")
        qk_ready = sem("qk_ready")
        logit_max = sem("logit_max")
        exps = sem("exps")
        attn_ready = sem("attn_ready")
        y_ready = sem("y_ready")
        yT_ready = sem("yT_ready")
        z_ready = sem("z_ready")
        score_used = sem("score_used")
        idx_ready = sem("idx_ready")
        best_ready = sem("best_ready")
        best_exp = sem("best_exp")
        lam_sum = sem("lam_sum")
        lam_exp = sem("lam_exp")
        idx_copied = sem("idx_copied")
        u_in = [sem(f"u_in{i}") for i in range(RING)]
        v_in = [sem(f"v_in{i}") for i in range(RING)]
        gather_turn = sem("gather_turn")
        dot_done = sem("dot_done")
        gelu_step = sem("gelu_step")
        gelu_arg = sem("gelu_arg")
        gelu_exp = sem("gelu_exp")
        weight_ready = sem("weight_ready")
        diag_ready = sem("diag_ready")
        v_used = sem("v_used")
        acc_read = sem("acc_read")
        h_done = sem("h_done")
        out_done = sem("out_done")
        dve_step = sem("dve_step")
        pool_step = sem("pool_step")

        x_dram = x.rearrange("a (b p) d -> (a b) p d", p=P)
        out_dram = out.rearrange("a (b p) d -> (a b) p d", p=P)
        u_dram = peer_u.rearrange("l e d -> (l e) d")
        v_dram = peer_v.rearrange("l e d -> (l e) d")
        zT = kT[:, 0:KT * (SEQ + 2)].rearrange("p (c t) -> p c t", c=KT)
        kTh = kT[:, 0:HEADS * SEQ].rearrange("p (h t) -> p h t", h=HEADS)
        in_dram = [w_qkv[0], conv_w_in[0]]
        out_w_dram = [w_o[0], conv_w_out[0]]

        def chunk_of(matrix, c):
            return matrix.rearrange("(k p) n -> p k n", p=P)[:, :, c * CHUNK:(c + 1) * CHUNK]

        x1T = diag
        xn1 = xf[:, 1, :]
        places = [wring[:, 0, :], wring[:, 1, :]] + [ring[:, :, :].rearrange("p r d -> p (r d)") for ring in (ring_u, ring_v)]
        places += [room[:, i, :] for i in range(len(KEPT))]

        def weights(n, what, c):
            if what == "in" and (n == 1 or n == 3 and c in KEPT):
                n -= 1
            place, before = held_at[(n, what, c)]
            return places[place], w_in[place], 16 * (before + 1)

        def by_row(place):
            return place.rearrange("p (k n) -> p k n", k=KT)

        def mixer_input(n):
            return (1, 2, 5, 7)[n]

        def expert_input(n):
            return (3, 4, 6, 8)[n]

        def copied(eng, pool, *keys):
            for key in keys:
                eng.wait_ge(pool.read_sem(*key), pool.times(*key) + 1)

        def written(eng, pool, *key):
            eng.wait_ge(pool.written_sem(*key), pool.times(*key) + 1)

        block = ctx.enter_context(nc.Block())

        @block.sync
        def _(sp):
            def load(n, what, c):
                place, landed, _ = weights(n, what, c)
                if what == "keys":
                    dst = place[:, 0:2 * PH * P].rearrange("p (k d) -> p k d", d=P)
                    src = peer_keys[n // 2].rearrange("h s k d -> k (h s) d")
                else:
                    matrix = {"in": in_dram[n // 2], "out": out_w_dram[n // 2], "wq": peer_w_q[n // 2]}[what]
                    dst, src = by_row(place), chunk_of(matrix, c)
                sp.dma_start(dst, src).then_inc(landed, 16)

            sp.dma_start(h[:, 0, :], x_dram[0]).then_inc(x_in[0], 16)
            sp.dma_start(gain_mix[:, :], norm_mix[0:1, :].partition_broadcast(P)).then_inc(mix_gain_in, 16)
            last = {}
            for n, what, c, place in loads:
                if (n, what, c) == (0, "in", 1):
                    sp.wait_ge(small_in, SMALL * 16)
                if place >= 4:
                    written(sp, pp, 1, "pv1")
                elif place in last:
                    m, was, at = last[place]
                    if was == "keys":
                        written(sp, tt, m, "keys3")
                    else:
                        written(sp, pp, 1 if m == 0 and was == "in" else m, f"{was}{at}")
                last[place] = n, what, c
                load(n, what, c)
            for b in range(2):
                sp.wait_ge(h_done, b + 1)
                sp.dma_start(out_dram[b], h[:, b, :]).then_inc(out_done, 16)
            sp.wait_ge(out_done, 32)

        @block.gpsimd
        def _(pool):
            nc.gpsimd.memset(ident[:, :], 0.0).then_inc(pool_step, 1)
            pool.wait_ge(pool_step, 1)
            nc.gpsimd.affine_select(out=ident[:, :], in_=ident[:, :], compare_op=ALU.not_equal, fill=1.0, base=0,
                                    pattern=[[-1, P]], channel_multiplier=1).then_inc(ident_made, 1)
            nc.gpsimd.memset(reverse[:, :], 0.0).then_inc(pool_step, 1)
            pool.wait_ge(pool_step, 2)
            nc.gpsimd.affine_select(out=reverse[:, :], in_=reverse[:, :], compare_op=ALU.not_equal, fill=1.0, base=1 - P,
                                    pattern=[[1, P]], channel_multiplier=1).then_inc(ident_made, 1)
            nc.gpsimd.iota(iota_i[:, :], [[1, TOPK]], base=0, channel_multiplier=0).then_inc(consts_made, 1)

            def gather(table, ring, used, landed, slot_no, first, column):
                if not (first and slot_no < RING):
                    pool.wait_ge(used, slot_no - (RING - 1))
                    if not isinstance(slot_no, int):
                        pool.sem_inc(gather_turn, 1)
                r = column % RING
                nc.gpsimd.indirect_dma_start(
                    ring[:, r, :], None, table,
                    bass.IndirectOffsetOnAxis(idx_now[:, column // 32, column % 32:column % 32 + 1], 0),
                ).then_inc(landed[r], 16)

            def quarter_windows(pair, first):
                for q in range(2):
                    pool.wait_ge(idx_ready, 2 * pair + (q + 1))
                    if not first:
                        for r in range(RING):
                            pool.wait_ge(v_in[r], 16 * 16 * pair + 128 * (q - 2) + 128)
                    nc.gpsimd.tensor_copy(idx_now[:, q, :], idx[:, bass.ds(64 * pair + 32 * q, 32)]).then_inc(idx_copied, 1)
                    pool.wait_ge(idx_copied, 2 * pair + (q + 1))
                    for s in range(4):
                        for j in range(GROUP):
                            column = 32 * q + GROUP * s + j
                            gather(u_dram, ring_u, dot_done, u_in, 64 * pair + column, first, column)
                            if not (first and column < GROUP):
                                gather(v_dram, ring_v, v_used, v_in, 64 * pair + (column - GROUP), first,
                                       (column - GROUP) % 64)

            quarter_windows(0, True)
            with nc.gpsimd.Fori(1, WINDOWS * SLOTS // 64) as pair:
                quarter_windows(pair, False)
            for j in range(GROUP):
                last = WINDOWS * SLOTS - GROUP + j
                gather(v_dram, ring_v, v_used, v_in, last, False, 64 - GROUP + j)

        @block.tensor
        def _(pe):
            def take(pool, *key):
                if pool.times(*key):
                    pe.wait_ge(pool.read_sem(*key), pool.times(*key))
                return pool.bank(*key)

            def project(n, what, c, src):
                place, landed, count = weights(n, what, c)
                pe.wait_ge(landed, count)
                use = f"{what}{c}"
                bank = take(pp, n, use)
                for k in range(KT):
                    mm = nc.tensor.matmul(bank[:, :], src[:, k, :], by_row(place)[:, k, :], start=(k == 0), stop=(k == KT - 1))
                mm.then_inc(pp.written_sem(n, use), 1)

            def transpose4(n, use, tiles):
                bank = take(tt, n, use)
                for j, tile in enumerate(tiles):
                    t = nc.tensor.transpose(bank[:, j * P:(j + 1) * P], tile, ident[:, :])
                t.then_inc(tt.written_sem(n, use), 1)

            def tiles(src, first):
                return [src[:, (first + j) * P:(first + j + 1) * P] for j in range(4)]

            def logits(n, pair):
                nk = (n + 1) * P
                for m in range(2):
                    use = f"logits{pair}{m}"
                    bank = take(ss, n, use)
                    for i in range(2):
                        mm = nc.tensor.matmul(bank[:, i * SEQ:i * SEQ + nk], qTa[m * DH:(m + 1) * DH, 2 * pair + i, :],
                                              kTh[m * DH:(m + 1) * DH, 2 * pair + i, 0:nk], start=True, stop=True)
                    mm.then_inc(ss.written_sem(n, use), 1)

            def turn_attention(n, c):
                pe.wait_ge(attn_ready, 2 * n + c + 1)
                for kb in range(n + 1):
                    transpose4(n, f"attn{c}{kb}", [attn[:, i, kb * P:(kb + 1) * P] for i in range(4)])

            def mix_values(n, c):
                copied(pe, tt, *((n, f"attn{c}{kb}") for kb in range(n + 1)))
                copied(pe, pp, *((m, f"in{k}") for m in range(n + 1) for k in (4, 5)))
                bank = take(pp, n, f"pv{c}")
                for i in range(4):
                    head = 4 * c + i
                    for kb in range(n + 1):
                        mm = nc.tensor.matmul(bank[:, i * P:(i + 1) * P], aT[:, kb, i, :],
                                              vrows[:, kb, head * P:(head + 1) * P], start=(kb == 0), stop=(kb == n))
                mm.then_inc(pp.written_sem(n, f"pv{c}"), 1)

            def turn_input(n, src):
                pe.wait_ge(xn_ready, mixer_input(n))
                for c in range(2):
                    transpose4(n, f"x{c}", tiles(src, 4 * c))
                copied(pe, tt, (n, "x0"), (n, "x1"))

            def start():
                pe.wait_ge(small_in, SMALL * 16)
                nc.tensor.transpose(take(tt, 0, "convw")[:, 0:24], cw_rows[:, :], ident[0:24, 0:24]).then_inc(
                    tt.written_sem(0, "convw"), 1)
                pe.wait_ge(dve_step, 1)
                nc.tensor.matmul(take(tt, 0, "bias")[0:HEADS, 0:FAR + 1], rel[:, :], hot, start=True, stop=True).then_inc(
                    tt.written_sem(0, "bias"), 1)

            def side(n, q):
                layer, b = divmod(n, 2)
                mix_q = q + SOONER[n]
                if q == 2 and n != 1:
                    turn_input(n, xn)
                if 2 <= q <= 7 and (layer == 1 or n == 0 and q <= 5):
                    project(n, "in", q - 2, xT)
                if q == 2 and n == 0:
                    start()
                if q == 6 and n == 0:
                    turn_input(1, xn1)
                if q == 7 and n == 0:
                    pe.wait_ge(bias_in, 16)
                    pe.wait_ge(ident_made, 2)
                    for c in range(4):
                        bank = take(tt, n, f"spread{c}")
                        nc.tensor.matmul(bank[:, :], reverse[:, :], ex[:, 2 * c:2 * c + 2, :].rearrange("p h k -> p (h k)"),
                                         start=True, stop=True).then_inc(tt.written_sem(n, f"spread{c}"), 1)
                if n == 0:
                    for c in {6: [0], 7: [1]}.get(q, []):
                        project(1, "in", c, x1T)
                if mix_q == 8 and layer == 0:
                    pe.wait_ge(qk_ready, n + 1)
                    for part, first in (("q", 0), ("k", KT)):
                        for c in range(2):
                            transpose4(n, f"{part}{c}", tiles(rows1 if n else rows, first + 4 * c))
                if q == 9 and layer == 1:
                    pe.wait_ge(z_ready, b + 1)
                    for part, first in (("z", KT), ("g", 0)):
                        for c in range(2):
                            transpose4(n, f"{part}{c}", tiles(rows, first + 4 * c))
                if layer == 0:
                    if mix_q in (9, 10, 12, 13):
                        if mix_q == 9:
                            copied(pe, tt, *((n, f"{part}{k}") for part in "qk" for k in range(2)))
                        logits(n, {9: 0, 10: 1, 12: 2, 13: 3}[mix_q])
                        if n == 0 and mix_q == 10:
                            project(0, "in", 4, xT)
                            project(0, "in", 5, xT)
                    if mix_q in (13, 16):
                        turn_attention(n, (mix_q - 13) // 3)
                    if mix_q in (14, 17):
                        mix_values(n, (mix_q - 14) // 3)
                        if n == 0:
                            for c in ((2,) if q == 14 else (3, 4)):
                                project(1, "in", c, x1T)
                if mix_q == 19 and layer == 0:
                    pe.wait_ge(y_ready, n + 1)
                    for c in range(2):
                        transpose4(n, f"y{c}", tiles(rows, 4 * c))
                if q == OUT_AT[n]:
                    if layer == 0:
                        copied(pe, tt, (n, "y0"), (n, "y1"))
                    else:
                        pe.wait_ge(yT_ready, b + 1)
                    project(n, "out", 0, yT)
                if q == OUT_AT[n] + 1:
                    project(n, "out", 1, yT)
                    if n == 0:
                        project(1, "in", 5, x1T)
                if q == KEYS_TURNED.get(n):
                    place, landed, count = weights(n, "keys", 0)
                    pe.wait_ge(landed, count)
                    for c in range(4):
                        transpose4(n, f"keys{c}", tiles(place, 4 * c))
                if q == min(PROJECT_AT[n]):
                    pe.wait_ge(xn_ready, expert_input(n))
                    for c in range(2):
                        transpose4(n, f"f{c}", tiles(xf[:, b, :], 4 * c))
                    copied(pe, tt, (n, "f0"), (n, "f1"))
                if q in SCORE_AT[n]:
                    c = SCORE_AT[n][q]
                    copied(pe, pp, (n, f"wq{c}"))
                    transpose4(n, f"qt{c}", tiles(rows, 4 * c))
                    copied(pe, tt, (n, f"qt{c}"), (2 * layer, f"keys{c}"))
                    bank = take(ss, n, f"score{c}")
                    for j in range(4):
                        mm = nc.tensor.matmul(bank[:, j * P:(j + 1) * P], qT[:, j, :], keysT[:, 4 * c + j, :], start=True, stop=True)
                    mm.then_inc(ss.written_sem(n, f"score{c}"), 1)
                if q in PROJECT_AT[n]:
                    project(n, "wq", PROJECT_AT[n][q], xT)

            def add_experts(group, slots, first, last):
                for j in slots:
                    pe.wait_ge(v_in[j % RING], group * 32 + 16 * (j // RING + 1))
                    pe.wait_ge(diag_ready, group * GROUP + (j + 1))
                    for half in range(2):
                        mm = nc.tensor.matmul(acc[half][:, :], diag[:, j, :], ring_v[:, j % RING, half * 512:(half + 1) * 512],
                                              start=(first and j == 0), stop=(last and j == GROUP - 1))
                    mm.then_inc(v_used, 1)

            def step(s, half):
                if s > 0:
                    g = s - 1
                    if g % GROUPS == 0 and g and half == 0:
                        pe.wait_ge(acc_read, g // GROUPS)
                    add_experts(g, HALVES[half], g % GROUPS == 0, g % GROUPS == GROUPS - 1)

            pe.wait_ge(ident_made, 1)
            for q in range(TICKS - LATE):
                side(0, q)
            for tick in range(BUSY):
                step(tick // 2, tick % 2)
                n, q = divmod(tick + TICKS - LATE, TICKS)
                if n < WINDOWS:
                    side(n, q)
            alone = BUSY // 2
            with nc.tensor.Fori(alone - 1, WINDOWS * GROUPS - 1) as group:
                add_experts(group, range(GROUP), False, False)
            add_experts(WINDOWS * GROUPS - 1, range(GROUP), False, True)

        @block.scalar
        def _(act):
            def start():
                act.wait_ge(lam_sum, 2)
                nc.scalar.activation(lam_s[:, :], lam_s[:, :], ACT.Exp).then_inc(lam_exp, 1)
                act.wait_ge(consts_made, 4)
                act.dma_start(bias_dram, bias_rows).then_inc(bias_out, 16)
                act.wait_ge(bias_out, 16)
                spread = bass.AP(tensor=bias_dram.tensor, offset=0, ap=[[1, P], [FAR + 1, HEADS], [1, SEQ]])
                act.dma_start(ex[:, :, :], spread).then_inc(bias_in, 16)

            def side(n, q):
                layer, b = divmod(n, 2)
                mix_q = q + SOONER[n]

                def copy(pool, use, dst, scale=1.0, of=n):
                    written(act, pool, of, use)
                    src = pool.bank(of, use)[:, :]
                    if len(dst.shape) == 3:
                        src = src.rearrange("p (a c) -> p a c", a=4)
                    nc.scalar.activation(dst, src, ACT.Copy, scale=scale).then_inc(pool.read_sem(of, use), 1)

                if q == 2 and n != 1:
                    for c in range(2):
                        copy(tt, f"x{c}", xT[:, 4 * c:4 * c + 4, :])
                if 2 <= q <= 7 and (layer == 1 or n == 0 and q <= 5):
                    copy(pp, f"in{q - 2}", rows[:, (q - 2) * CHUNK:(q - 1) * CHUNK])
                if q == 2 and n == 0:
                    start()
                if q == 6 and n == 0:
                    for c in range(2):
                        copy(tt, f"x{c}", x1T[:, 4 * c:4 * c + 4, :], of=1)
                if n == 0:
                    for c in {6: [0], 7: [1]}.get(q, []):
                        copy(pp, f"in{c}", rows1[:, c * CHUNK:(c + 1) * CHUNK], of=1)
                if mix_q == 8 and layer == 0:
                    act.wait_ge(consts_made, 3)
                    for c in range(2):
                        copy(tt, f"q{c}", qTa[:, 4 * c:4 * c + 4, :], qg[:, 0:1])
                    for c in range(2):
                        copy(tt, f"k{c}", kTh[:, 4 * c:4 * c + 4, b * P:(b + 1) * P], qg[:, 1:2])
                if q == 9 and layer == 1:
                    for c in range(2):
                        copy(tt, f"z{c}", zT[:, 4 * c:4 * c + 4, 2 + b * P:2 + (b + 1) * P])
                    for c in range(2):
                        copy(tt, f"g{c}", qTa[:, 4 * c:4 * c + 4, :])
                if layer == 0:
                    if mix_q in (14, 17):
                        c = (mix_q - 14) // 3
                        copy(pp, f"pv{c}", rows[:, c * CHUNK:(c + 1) * CHUNK])
                    if mix_q in (11, 14):
                        c = (mix_q - 11) // 3
                        nk = (b + 1) * P
                        act.wait_ge(logit_max, 2 * n + c + 1)
                        for i in range(8):
                            nc.scalar.activation(ex[:, i, 0:nk], ex[:, i, 0:nk], ACT.Exp, bias=mx[:, i:i + 1],
                                                 accum_out=sums[:, i:i + 1]).then_inc(exps, 1)
                    if n == 0 and q == 11:
                        for c in range(2):
                            copy(pp, f"in{4 + c}", vrows[:, 0, c * CHUNK:(c + 1) * CHUNK])
                    if n == 0:
                        for c in {14: (2,), 17: (3, 4), 20: (5,)}.get(q, ()):
                            copy(pp, f"in{c}", rows1[:, c * CHUNK:(c + 1) * CHUNK] if c < 4 else
                                 vrows[:, 1, (c - 4) * CHUNK:(c - 3) * CHUNK], of=1)
                    if mix_q in (13, 16):
                        c = (mix_q - 13) // 3
                        for kb in range(b + 1):
                            copy(tt, f"attn{c}{kb}", aT[:, kb, :, :])
                    if mix_q == 19:
                        for c in range(2):
                            copy(tt, f"y{c}", yT[:, 4 * c:4 * c + 4, :])
                if q == KEYS_TURNED.get(n):
                    for c in range(4):
                        copy(tt, f"keys{c}", keysT[:, 4 * c:4 * c + 4, :])
                if q == min(PROJECT_AT[n]):
                    for c in range(2):
                        copy(tt, f"f{c}", xT[:, 4 * c:4 * c + 4, :])
                if q in SCORE_AT[n]:
                    c = SCORE_AT[n][q]
                    copy(tt, f"qt{c}", qT[:, :, :])
                    if 4 * n + c >= 2:
                        act.wait_ge(score_used, 4 * n + c - 1)
                    copy(ss, f"score{c}", score[:, c % 2, :, :])
                if q in PROJECT_AT[n]:
                    c = PROJECT_AT[n][q]
                    copy(pp, f"wq{c}", rows[:, c * CHUNK:(c + 1) * CHUNK])
                if q in RANKED_AT[n]:
                    c = RANKED_AT[n][q]
                    act.wait_ge(best_ready, 4 * n + c + 1)
                    nc.scalar.activation(best_e[:, :, :], best_e[:, :, :], ACT.Exp).then_inc(best_exp, 1)

            def step(s):
                act.wait_ge(gelu_arg, s + 1)
                nc.scalar.activation(gelu_e[:, :], gelu_b[:, :], ACT.Exp, scale=-2.0 * GELU_C).then_inc(gelu_exp, 1)
                act.wait_ge(weight_ready, s + 1)
                for j in range(GROUP):
                    if not (isinstance(s, int) and s == 0):
                        act.wait_ge(v_used, s * GROUP + (j + 1 - GROUP))
                    nc.scalar.activation(diag[:, j, :], ident[:, :], ACT.Copy, scale=weight[:, j:j + 1]).then_inc(diag_ready, 1)

            act.dma_start(h[:, 1, :], x_dram[1]).then_inc(x_in[1], 16)
            small = [(hot, one_hot), (rel[0:BUCKETS, :], rel_bias),
                     (cw_rows[:, :], conv_w[0].rearrange("w (c p) -> (w c) p", p=P)),
                     (subg[:, :], sub_gain[0:1, :].partition_broadcast(P))]
            small += [(lam4[:, i, :], v[0:1, :].partition_broadcast(P)) for i, v in enumerate((lam_q1, lam_k1, lam_q2, lam_k2))]
            for i, gain in enumerate((q_gain, k_gain)):
                for m in range(2):
                    small.append((qg[m * DH:(m + 1) * DH, i:i + 1], gain[0:1, :].rearrange("a d -> d a")))
            assert len(small) == SMALL
            for dst, src in small:
                act.dma_start(dst, src).then_inc(small_in, 16)
            act.dma_start(gain_ffn[:, :], norm_ffn[0:1, :].partition_broadcast(P)).then_inc(ffn_gain_in, 16)
            for q in range(TICKS - LATE):
                side(0, q)
            for tick in range(BUSY):
                if tick % 2:
                    step(tick // 2)
                n, q = divmod(tick + TICKS - LATE, TICKS)
                if q < TAIL:
                    side(n - 1, q + TICKS)
                if n < WINDOWS:
                    side(n, q)
                if n == 2 and q == 0:
                    act.wait_ge(xn_ready, 4)
                    act.dma_start(gain_mix[:, :], norm_mix[1:2, :].partition_broadcast(P)).then_inc(mix_gain_in, 16)
                    act.dma_start(gain_ffn[:, :], norm_ffn[1:2, :].partition_broadcast(P)).then_inc(ffn_gain_in, 16)
            alone = BUSY // 2
            with nc.scalar.Fori(alone, WINDOWS * GROUPS) as s:
                step(s)

        @block.vector
        def _(dve):
            done = [0]

            def link(ins):
                done[0] += 1
                ins.then_inc(dve_step, 1)
                dve.wait_ge(dve_step, done[0])

            def rms(src3, count, dim):
                sq = scratch[:, 0:count * dim].rearrange("p (c d) -> p c d", d=dim)
                if count == 1:
                    link(nc.vector.tensor_tensor_reduce(sq[:, 0, :], src3[:, 0, :], src3[:, 0, :], 1.0, 0.0, ALU.mult, ALU.add,
                                                        stat[:, 0:1]))
                else:
                    link(nc.vector.tensor_tensor(sq, src3, src3, ALU.mult))
                    link(nc.vector.tensor_reduce(stat[:, 0:count], sq, AX.X, ALU.add))
                link(nc.vector.tensor_scalar(stat[:, 0:count], stat[:, 0:count], 1.0 / dim, EPS, ALU.mult, ALU.add))
                v, y, t = stat[:, 0:count], root[:, 0:count], root_t[:, 0:count]
                link(nc.vector.tensor_scalar(y.bitcast(U32), v.bitcast(U32), 1, None, ALU.logical_shift_right))
                link(nc.vector.tensor_scalar(y.bitcast(U32), y.bitcast(U32), -1.0, float(0x5F3759DF), ALU.mult, ALU.add))
                for _ in range(3):
                    link(nc.vector.tensor_tensor(t, y, y, ALU.mult))
                    link(nc.vector.tensor_tensor(t, t, v, ALU.mult))
                    link(nc.vector.tensor_scalar(t, t, -0.5, 1.5, ALU.mult, ALU.add))
                    link(nc.vector.tensor_tensor(y, y, t, ALU.mult))

            def norm(b, gain, dst):
                rms(h[:, b:b + 1, :], 1, D)
                link(nc.vector.scalar_tensor_tensor(out=dst, in0=h[:, b, :], scalar=root[:, 0:1], in1=gain[:, :],
                                                    op0=ALU.mult, op1=ALU.mult))
                dve.sem_inc(xn_ready, 1)

            def finish(window):
                b = window % 2
                dve.wait_ge(v_used, SLOTS * (window + 1))
                for half in range(2):
                    hh = h[:, b, half * 512:(half + 1) * 512]
                    link(nc.vector.tensor_tensor(hh, hh, acc[half][:, :], ALU.add))
                dve.sem_inc(acc_read, 1)
                if window >= WINDOWS - 2:
                    dve.sem_inc(h_done, 1)

            def norm_queries(n):
                copied(dve, pp, *((n, f"in{c}") for c in range(4)))
                qk = (rows1 if n else rows)[:, 0:2 * D].rearrange("p (c d) -> p c d", d=DH)
                rms(qk, 32, DH)
                link(nc.vector.tensor_tensor(qk, qk, root[:, 0:32].unsqueeze(2).to_broadcast([P, 32, DH]), ALU.mult))
                dve.sem_inc(qk_ready, 1)

            def add_bias(n, pair):
                nk = (n + 1) * P
                first_key = SEQ - nk
                for m in range(2):
                    key = (n, f"logits{pair}{m}")
                    written(dve, ss, *key)
                    src = ss.bank(*key)[:, :].rearrange("p (i k) -> p i k", i=2)[:, :, 0:nk]
                    at = 4 * (pair % 2) + m
                    link(nc.vector.tensor_tensor(ex[:, at:at + 3:2, 0:nk], src,
                                                 bias[:, 2 * pair:2 * pair + 2, first_key:first_key + nk], ALU.add))
                    dve.sem_inc(ss.read_sem(*key), 1)

            def negative_max(n):
                link(nc.vector.tensor_reduce(mx[:, :], ex[:, :, 0:(n + 1) * P], AX.X, ALU.max))
                link(nc.vector.tensor_scalar(mx[:, :], mx[:, :], -1.0, None, ALU.mult))
                dve.sem_inc(logit_max, 1)

            def difference(n, c):
                nk = (n + 1) * P
                dve.wait_ge(exps, 8 * (2 * n + c + 1))
                link(nc.vector.reciprocal(sums[:, :], sums[:, :]))
                second = sums[:, :].rearrange("p (i m) -> p i m", m=2)[:, :, 1]
                link(nc.vector.tensor_scalar(second, second, neg_lam[:, 0:1], None, ALU.mult))
                for i in range(4):
                    last = nc.vector.tensor_scalar(ex[:, 2 * i + 1, 0:nk], ex[:, 2 * i + 1, 0:nk], sums[:, 2 * i + 1:2 * i + 2], None, ALU.mult)
                link(last)
                for i in range(4):
                    last = nc.vector.scalar_tensor_tensor(out=attn[:, i, 0:nk], in0=ex[:, 2 * i, 0:nk], scalar=sums[:, 2 * i:2 * i + 1],
                                                          in1=ex[:, 2 * i + 1, 0:nk], op0=ALU.mult, op1=ALU.add)
                link(last)
                dve.sem_inc(attn_ready, 1)

            def convolve(b):
                copied(dve, tt, *((2 + b, f"{part}{k}") for part in "zg" for k in range(2)))
                a = scratch[:, 0:D].rearrange("p (c t) -> p c t", c=KT)
                t = scratch[:, D:2 * D].rearrange("p (c t) -> p c t", c=KT)
                for w in range(3):
                    tap = cw[:, w * KT:(w + 1) * KT].unsqueeze(2).to_broadcast([P, KT, P])
                    link(nc.vector.tensor_tensor(a if w == 0 else t, zT[:, :, b * P + w:b * P + w + P], tap, ALU.mult))
                    if w:
                        link(nc.vector.tensor_tensor(a, a, t, ALU.add))
                link(nc.vector.tensor_tensor(yT[:, :, :], a, qTa[:, :, :], ALU.mult))
                dve.sem_inc(yT_ready, 1)

            def top16(values, tops, indices):
                for v, t in zip(values, tops):
                    last = nc.vector.max(t[:, 0:8], v)
                link(last)
                for v, t, i in zip(values, tops, indices):
                    last = nc.vector.max_index(i[:, 0:8], t[:, 0:8], v)
                link(last)
                for v, t in zip(values, tops):
                    last = nc.vector.match_replace(v, t[:, 0:8], v, LOW)
                link(last)
                for v, t in zip(values, tops):
                    last = nc.vector.max(t[:, 8:16], v)
                link(last)
                for v, t, i in zip(values, tops, indices):
                    last = nc.vector.max_index(i[:, 8:16], t[:, 8:16], v)
                link(last)

            def best_keys(n, c):
                copied(dve, ss, (n, f"score{c}"))
                hp = range(4 * c, 4 * c + 4)
                top16([score[:, c % 2, j, :] for j in range(4)], [top[:, k, :] for k in hp], [top_i[:, k, :] for k in hp])
                dve.sem_inc(score_used, 1)
                link(nc.vector.tensor_copy(top_f[:, 4 * c:4 * c + 4, :], top_i[:, 4 * c:4 * c + 4, :]))

            def best_pairs(n, c):
                for j in range(2):
                    s0 = top[:, 4 * c + 2 * j, :].unsqueeze(2).to_broadcast([P, TOPK, TOPK])
                    s1 = top[:, 4 * c + 2 * j + 1, :].unsqueeze(1).to_broadcast([P, TOPK, TOPK])
                    link(nc.vector.tensor_tensor(cand[:, j, :, :], s0, s1, ALU.add))
                flat = [cand[:, j, :, :].rearrange("p a c -> p (a c)") for j in range(2)]
                top16(flat, [best[:, 2 * c + j, :] for j in range(2)], [pos[:, j * TOPK:(j + 1) * TOPK] for j in range(2)])

            def find_rows(n, c):
                layer = n // 2
                link(nc.vector.tensor_scalar(pos2[:, 0, :], pos[:, :], 4, None, ALU.logical_shift_right))
                link(nc.vector.tensor_scalar(pos2[:, 1, :], pos[:, :], TOPK - 1, None, ALU.bitwise_and))
                link(nc.vector.tensor_copy(pos_f[:, :, :], pos2[:, :, :]))
                for side_no in range(2):
                    one = pick[:, :, :].rearrange("p j (k a) -> p (j k) a", a=TOPK)
                    link(nc.vector.tensor_tensor(one, pos_f[:, side_no, :].unsqueeze(2).to_broadcast([P, 2 * TOPK, TOPK]),
                                                 iota_f[:, :].unsqueeze(1).to_broadcast([P, 2 * TOPK, TOPK]), ALU.is_equal))
                    for j in range(2):
                        p3 = pick[:, j, :].rearrange("p (k a) -> p k a", a=TOPK)
                        choice = top_f[:, 4 * c + 2 * j + side_no, :].unsqueeze(1).to_broadcast([P, TOPK, TOPK])
                        link(nc.vector.tensor_tensor(p3, p3, choice, ALU.mult))
                    link(nc.vector.tensor_reduce(row_f[:, side_no, :], one, AX.X, ALU.add))
                link(nc.vector.tensor_scalar(idx_f[:, :], row_f[:, 0, :], float(NKEYS), float(layer * EXPERTS), ALU.mult, ALU.add))
                link(nc.vector.tensor_tensor(idx_f[:, :], idx_f[:, :], row_f[:, 1, :], ALU.add))
                at = n * SLOTS + c * 2 * TOPK
                link(nc.vector.tensor_copy(idx[:, at:at + 2 * TOPK], idx_f[:, :]))
                dve.sem_inc(idx_ready, 1)

            def gate(n, c):
                pair = best[:, 2 * c:2 * c + 2, :]
                link(nc.vector.tensor_tensor(best_e[:, :, :], pair, pair[:, :, 0:1].to_broadcast([P, 2, TOPK]), ALU.subtract))
                dve.sem_inc(best_ready, 1)
                dve.wait_ge(best_exp, 4 * n + c + 1)
                link(nc.vector.tensor_reduce(best_s[:, :], best_e[:, :, :], AX.X, ALU.add))
                link(nc.vector.reciprocal(best_s[:, :], best_s[:, :]))
                at = n * SLOTS + c * 2 * TOPK
                g3 = gates[:, at:at + 2 * TOPK].rearrange("p (h k) -> p h k", h=2)
                link(nc.vector.tensor_tensor(g3, best_e[:, :, :], best_s[:, :].unsqueeze(2).to_broadcast([P, 2, TOPK]), ALU.mult))

            def start():
                dve.wait_ge(consts_made, 1)
                dve.wait_ge(small_in, SMALL * 16)
                link(nc.vector.tensor_copy(iota_f[:, :], iota_i[:, :]))
                dve.sem_inc(consts_made, 1)
                link(nc.vector.tensor_scalar(qg[:, 0:1], qg[:, 0:1], DH ** -0.5, None, ALU.mult))
                dve.sem_inc(consts_made, 1)
                link(nc.vector.tensor_scalar(subg[:, :], subg[:, :], 1.0 - LAM_INIT, None, ALU.mult))
                for i in range(2):
                    pair = lam4[:, 2 * i, :]
                    link(nc.vector.tensor_tensor(pair, pair, lam4[:, 2 * i + 1, :], ALU.mult))
                    link(nc.vector.tensor_reduce(lam_s[:, i:i + 1], pair, AX.X, ALU.add))
                    dve.sem_inc(lam_sum, 1)
                dve.wait_ge(lam_exp, 1)
                link(nc.vector.tensor_tensor(neg_lam[:, :], lam_s[:, 1:2], lam_s[:, 0:1], ALU.subtract))
                link(nc.vector.tensor_scalar(neg_lam[:, :], neg_lam[:, :], -LAM_INIT, None, ALU.add))
                written(dve, tt, 0, "convw")
                link(nc.vector.tensor_copy(cw[:, :], tt.bank(0, "convw")[:, 0:24]))
                dve.sem_inc(tt.read_sem(0, "convw"), 1)
                written(dve, tt, 0, "bias")
                link(nc.vector.tensor_copy(bias_rows, tt.bank(0, "bias")[0:HEADS, 0:FAR + 1]))
                dve.sem_inc(tt.read_sem(0, "bias"), 1)
                dve.sem_inc(consts_made, 1)

            def side(n, q):
                layer, b = divmod(n, 2)
                mix_q = q + SOONER[n]
                if q == 1 and n != 1:
                    if n == 0:
                        dve.wait_ge(x_in[0], 16)
                    dve.wait_ge(mix_gain_in, 16 * (layer + 1))
                    norm(b, gain_mix, xn[:, :])
                    if n == 0:
                        start()
                        dve.wait_ge(x_in[1], 16)
                        norm(1, gain_mix, xn1)
                if q == 7 and n == 0:
                    for c in range(4):
                        key = (n, f"spread{c}")
                        written(dve, tt, *key)
                        link(nc.vector.tensor_copy(bias[:, 2 * c:2 * c + 2, :].rearrange("p h k -> p (h k)"), tt.bank(*key)[:, :]))
                        dve.sem_inc(tt.read_sem(*key), 1)
                if layer == 0:
                    if n == 0 and q in (6, 20):
                        norm_queries((6, 20).index(q))
                    if mix_q in (10, 11, 13, 14):
                        add_bias(n, {10: 0, 11: 1, 13: 2, 14: 3}[mix_q])
                    if mix_q in (11, 14):
                        negative_max(n)
                    if mix_q in (12, 15):
                        difference(n, (mix_q - 12) // 3)
                    if mix_q == 18:
                        copied(dve, pp, (n, "pv0"), (n, "pv1"))
                        o3 = rows[:, 0:D].rearrange("p (h d) -> p h d", h=HEADS)
                        rms(o3, HEADS, P)
                        link(nc.vector.tensor_tensor(o3, o3, root[:, 0:HEADS].unsqueeze(2).to_broadcast([P, HEADS, P]), ALU.mult))
                        link(nc.vector.tensor_tensor(o3, o3, subg[:, :].unsqueeze(1).to_broadcast([P, HEADS, P]), ALU.mult))
                        dve.sem_inc(y_ready, 1)
                else:
                    if q == 8:
                        if b == 0:
                            link(nc.vector.memset(zT[:, :, 0:2], 0.0))
                        copied(dve, pp, *((n, f"in{c}") for c in range(2, 6)))
                        link(nc.vector.tensor_tensor(rows[:, D:2 * D], rows[:, D:2 * D], rows[:, 2 * D:3 * D], ALU.mult))
                        dve.sem_inc(z_ready, 1)
                    if q == 10:
                        convolve(b)
                if q == OUT_AT[n] + 2:
                    for c in range(2):
                        key = (n, f"out{c}")
                        written(dve, pp, *key)
                        hh = h[:, b, c * CHUNK:(c + 1) * CHUNK]
                        link(nc.vector.tensor_tensor(hh, hh, pp.bank(*key)[:, :], ALU.add))
                        dve.sem_inc(pp.read_sem(*key), 1)
                    dve.wait_ge(ffn_gain_in, 16 * (layer + 1))
                    norm(b, gain_ffn, xf[:, b, :])
                if q in KEYS_AT[n]:
                    best_keys(n, KEYS_AT[n][q])
                if q in PAIRS_AT[n]:
                    best_pairs(n, PAIRS_AT[n][q])
                if q in RANKED_AT[n]:
                    find_rows(n, RANKED_AT[n][q])
                    gate(n, RANKED_AT[n][q])

            def dot(s, b, slots):
                for j in slots:
                    dve.wait_ge(u_in[j % RING], s * 32 + 16 * (j // RING + 1))
                    row = ring_u[:, j % RING, :]
                    nc.vector.tensor_tensor_reduce(row, row, xf[:, b, :], 1.0, 0.0, ALU.mult, ALU.add,
                                                   dots[:, j:j + 1]).then_inc(dot_done, 1)

            def weigh(s):
                fresh = isinstance(s, int) and s == 0
                dve.wait_ge(dot_done, s * GROUP + GROUP)
                nc.vector.scalar_tensor_tensor(out=gelu_a[:, :], in0=dots[:, :], scalar=0.044715, in1=dots[:, :],
                                               op0=ALU.mult, op1=ALU.mult).then_inc(gelu_step, 1)
                dve.wait_ge(gelu_step, s * 5 + 1)
                nc.vector.scalar_tensor_tensor(out=gelu_b[:, :], in0=gelu_a[:, :], scalar=1.0, in1=dots[:, :],
                                               op0=ALU.add, op1=ALU.mult).then_inc(gelu_arg, 1)
                nc.vector.tensor_tensor(dots_g[:, :], dots[:, :], gates[:, bass.ds(s * GROUP, GROUP)], ALU.mult).then_inc(gelu_step, 1)
                dve.wait_ge(gelu_exp, s + 1)
                nc.vector.tensor_scalar(gelu_e[:, :], gelu_e[:, :], 1.0, None, ALU.add).then_inc(gelu_step, 1)
                dve.wait_ge(gelu_step, s * 5 + 3)
                nc.vector.reciprocal(gelu_e[:, :], gelu_e[:, :]).then_inc(gelu_step, 1)
                dve.wait_ge(gelu_step, s * 5 + 4)
                if not fresh:
                    dve.wait_ge(diag_ready, s * GROUP)
                nc.vector.tensor_tensor(weight[:, :], gelu_e[:, :], dots_g[:, :], ALU.mult).then_inc(gelu_step, 1)
                dve.wait_ge(gelu_step, s * 5 + 5)
                dve.sem_inc(weight_ready, 1)

            link(nc.vector.memset(rel[BUCKETS:BUCKETS + 1, :], MASKED))
            for q in range(TICKS - LATE):
                side(0, q)
            for tick in range(BUSY):
                s, half = divmod(tick, 2)
                dot(s, (s // GROUPS) % 2, HALVES[half])
                if half:
                    weigh(s)
                if tick % TICKS == 1 and s:
                    finish(s // GROUPS - 1)
                n, q = divmod(tick + TICKS - LATE, TICKS)
                if q < TAIL:
                    side(n - 1, q + TICKS)
                if n < WINDOWS:
                    side(n, q)
            alone = BUSY // 2
            with nc.vector.Fori(alone, WINDOWS * GROUPS) as s:
                dot(s, 1, range(GROUP))
                weigh(s)
            finish(WINDOWS - 1)


def at_ticks(first, later):
    return [{q: c for c, q in enumerate(first if n == 0 else later)} for n in range(WINDOWS)]


PROJECT_AT = at_ticks((22, 23, 25, 28), (17, 19, 22, 25))
SCORE_AT = at_ticks((23, 25, 28, 31), (18, 21, 24, 27))
KEYS_AT = at_ticks((24, 27, 30, 33), (19, 22, 25, 29))
PAIRS_AT = at_ticks((25, 28, 31, 34), (20, 23, 26, 30))
RANKED_AT = at_ticks((25, 29, 32, 35), (21, 24, 28, 31))
SOONER = (0, 6, 0, 0)
OUT_AT = (19, 14, 12, 12)
KEYS_TURNED = {0: 21, 2: 10}
BUSY = (WINDOWS - 1) * TICKS + LATE
HALVES = (range(0, GROUP // 2), range(GROUP // 2, GROUP))
SMALL = 12


_INS = ['x', 'rel_bias', 'norm_mix', 'norm_ffn', 'attn_w_qkv', 'attn_q_gain', 'attn_k_gain', 'attn_lam_q1', 'attn_lam_k1',
        'attn_lam_q2', 'attn_lam_k2', 'attn_sub_gain', 'attn_w_o', 'conv_w_in', 'conv_w', 'conv_w_out', 'peer_w_q',
        'peer_keys', 'peer_u', 'peer_v']


def kernel(**inputs):
    import concourse.bacc as bacc
    from concourse.bass_utils import run_bass_kernel_spmd

    nc = bacc.Bacc("TRN2", target_bir_lowering=False, num_devices=1)
    arrays, args = {}, []
    given = {name: np.ascontiguousarray(inputs[name]) for name in _INS}
    given["one_hot"] = bucket_one_hot()
    for name, a in given.items():
        arrays[f"in_{name}_dram"] = a
        args.append(nc.dram_tensor(f"in_{name}_dram", a.shape, mybir.dt.from_np(a.dtype), kind="ExternalInput").ap())
    out = nc.dram_tensor("out_0_dram", (1, SEQ, D), F32, kind="ExternalOutput").ap()
    build(nc, *args, out)
    r = run_bass_kernel_spmd(nc, [arrays], core_ids=[0])
    return r.results[0]["out_0_dram"]
```
